# Optimizing a Trainium2 kernel written in Bass

```python
import jax, jax.numpy as jnp
from jax import lax
import numpy as np

D_MODEL = 1024
BATCH = 1
SEQ = 512
DEPTH = 2
DEC_BATCH = 8
DEC_SEQ = 1
PAST_LEN = 2048
PAGE_SIZE = 128

PLE_DIM = 256
N_MIXERS = 2
N_A = (DEPTH + 1) // 2
N_B = DEPTH // 2
EPS = 1e-6

ML_HEADS = 4
ML_DV = D_MODEL // ML_HEADS
ML_DK = ML_DV // 2
ML_CHUNK = 64
ML_HK = ML_HEADS * ML_DK
ML_IN = 2 * ML_HK + 2 * D_MODEL + 2 * ML_HEADS
FORGET_BIAS = 3.0

SW_HEADS = 16
SW_KV_HEADS = 4
SW_HD = D_MODEL // SW_HEADS
SW_GROUP = SW_HEADS // SW_KV_HEADS
WINDOW = 128
SW_BLOCK = WINDOW
SW_IN = (SW_HEADS + 2 * SW_KV_HEADS) * SW_HD
ROPE_THETA = 10000.0

D_FF = 2816
CONV_W = 3

kernel_name = "hybrid_mlstm_swa_convffn_decode_step"

def rmsnorm(x, g):
    xf = x.astype(jnp.float32)
    y = xf * lax.rsqrt(jnp.mean(xf * xf, axis=-1, keepdims=True) + EPS)
    return (y * g.astype(jnp.float32)).astype(x.dtype)

def rope(x, pos):
    half = x.shape[-1] // 2
    inv = ROPE_THETA ** (-jnp.arange(half, dtype=jnp.float32) / half)
    ang = pos[:, None] * inv[None, :]
    cos = jnp.cos(ang)[None, :, None, :]
    sin = jnp.sin(ang)[None, :, None, :]
    xf = x.astype(jnp.float32)
    x1, x2 = xf[..., :half], xf[..., half:]
    return jnp.concatenate([x1 * cos - x2 * sin, x2 * cos + x1 * sin], axis=-1).astype(x.dtype)

def mlstm_chunk(carry, inp):
    C, n, m = carry
    q, k, v, ig, lf = inp
    L = q.shape[2]
    b = jnp.cumsum(lf, axis=-1)
    causal = jnp.tril(jnp.ones((L, L), dtype=bool))
    d = jnp.where(causal, b[..., :, None] - b[..., None, :] + ig[..., None, :], -jnp.inf)
    a = b + m[..., None]
    m_t = jnp.maximum(a, jnp.max(d, axis=-1))
    w_inter = jnp.exp(a - m_t)
    s = jnp.einsum('bhtk,bhsk->bhts', q, k) * jnp.exp(d - m_t[..., None])
    num = w_inter[..., None] * jnp.einsum('bhtk,bhkv->bhtv', q, C) + jnp.einsum('bhts,bhsv->bhtv', s, v)
    qn = w_inter * jnp.einsum('bhtk,bhk->bht', q, n) + jnp.sum(s, axis=-1)
    h = num / jnp.maximum(jnp.abs(qn), jnp.exp(-m_t))[..., None]
    bL = b[..., -1]
    g = bL[..., None] - b + ig
    m_new = jnp.maximum(bL + m, jnp.max(g, axis=-1))
    w_old = jnp.exp(bL + m - m_new)
    w_s = jnp.exp(g - m_new[..., None])
    C_new = w_old[..., None, None] * C + jnp.einsum('bhs,bhsk,bhsv->bhkv', w_s, k, v)
    n_new = w_old[..., None] * n + jnp.einsum('bhs,bhsk->bhk', w_s, k)
    return (C_new, n_new, m_new), h

def mlstm_mixer(xn, w_in, b_gate, w_out, state, chunk):
    B, T, _ = xn.shape
    proj = xn @ w_in
    f32 = jnp.float32
    q = proj[..., :ML_HK].astype(f32).reshape(B, T, ML_HEADS, ML_DK).transpose(0, 2, 1, 3) * (ML_DK ** -0.5)
    k = proj[..., ML_HK:2 * ML_HK].astype(f32).reshape(B, T, ML_HEADS, ML_DK).transpose(0, 2, 1, 3)
    v = proj[..., 2 * ML_HK:2 * ML_HK + D_MODEL].astype(f32).reshape(B, T, ML_HEADS, ML_DV).transpose(0, 2, 1, 3)
    o = proj[..., 2 * ML_HK + D_MODEL:2 * ML_HK + 2 * D_MODEL].astype(f32)
    gates = proj[..., 2 * ML_HK + 2 * D_MODEL:].astype(f32) + b_gate.astype(f32)
    ig = gates[..., :ML_HEADS].transpose(0, 2, 1)
    lf = jax.nn.log_sigmoid(gates[..., ML_HEADS:]).transpose(0, 2, 1)
    nc = T // chunk

    def to_chunks(a):
        a = a.reshape(a.shape[:2] + (nc, chunk) + a.shape[3:])
        return jnp.moveaxis(a, 2, 0)

    init = tuple(s.astype(f32) for s in state)
    (C, n, m), h = lax.scan(mlstm_chunk, init, (to_chunks(q), to_chunks(k), to_chunks(v), to_chunks(ig), to_chunks(lf)))
    h = jnp.moveaxis(h, 0, 2).reshape(B, ML_HEADS, T, ML_DV).transpose(0, 2, 1, 3).reshape(B, T, D_MODEL)
    y = (jax.nn.sigmoid(o) * h).astype(xn.dtype) @ w_out
    return y, (C.astype(xn.dtype), n.astype(xn.dtype), m.astype(xn.dtype))

def sink_probs(s, sinks):
    sk = sinks.astype(jnp.float32).reshape(SW_KV_HEADS, SW_GROUP)[..., None, None]
    mx = jnp.maximum(jnp.max(s, axis=-1, keepdims=True), sk)
    p = jnp.exp(s - mx)
    return p / (jnp.sum(p, axis=-1, keepdims=True) + jnp.exp(sk - mx))

def swa_qkv(xn, w_in, pos):
    B, T, _ = xn.shape
    proj = xn @ w_in
    q = proj[..., :SW_HEADS * SW_HD].reshape(B, T, SW_HEADS, SW_HD)
    k = proj[..., SW_HEADS * SW_HD:(SW_HEADS + SW_KV_HEADS) * SW_HD].reshape(B, T, SW_KV_HEADS, SW_HD)
    v = proj[..., (SW_HEADS + SW_KV_HEADS) * SW_HD:].reshape(B, T, SW_KV_HEADS, SW_HD)
    return rope(q, pos), rope(k, pos), v

def swa_prompt(xn, w_in, sinks, w_out):
    B, T, _ = xn.shape
    q, k, v = swa_qkv(xn, w_in, jnp.arange(T, dtype=jnp.float32))
    nb = T // SW_BLOCK
    qb = q.reshape(B, nb, SW_BLOCK, SW_KV_HEADS, SW_GROUP, SW_HD)
    kb = k.reshape(B, nb, SW_BLOCK, SW_KV_HEADS, SW_HD)
    vb = v.reshape(B, nb, SW_BLOCK, SW_KV_HEADS, SW_HD)
    pad = ((0, 0), (1, 0), (0, 0), (0, 0), (0, 0))
    kc = jnp.concatenate([jnp.pad(kb[:, :-1], pad), kb], axis=2)
    vc = jnp.concatenate([jnp.pad(vb[:, :-1], pad), vb], axis=2)
    s = jnp.einsum('bnqkgd,bnskd->bnkgqs', qb, kc).astype(jnp.float32) * (SW_HD ** -0.5)
    qi = jnp.arange(SW_BLOCK)[:, None] + SW_BLOCK
    si = jnp.arange(2 * SW_BLOCK)[None, :]
    diff = qi - si
    band = (diff >= 0) & (diff <= WINDOW)
    blk_ok = (jnp.arange(nb)[:, None, None] > 0) | (si[None] >= SW_BLOCK)
    mask = band[None] & blk_ok
    s = jnp.where(mask[None, :, None, None], s, -jnp.inf)
    p = sink_probs(s, sinks).astype(v.dtype)
    o = jnp.einsum('bnkgqs,bnskd->bnqkgd', p, vc).reshape(B, T, SW_HEADS * SW_HD)
    nkeep = min(WINDOW, T)
    return o @ w_out, k[:, T - nkeep:], v[:, T - nkeep:]

def swa_sample(xn, w_in, sinks, w_out, kbuf, vbuf):
    B, T, _ = xn.shape
    nbuf = kbuf.shape[1]
    qpos = PAST_LEN + jnp.arange(T, dtype=jnp.int32)
    q, k, v = swa_qkv(xn, w_in, qpos.astype(jnp.float32))
    kc = jnp.concatenate([kbuf.astype(k.dtype), k], axis=1)
    vc = jnp.concatenate([vbuf.astype(v.dtype), v], axis=1)
    kpos = jnp.concatenate([PAST_LEN - nbuf + jnp.arange(nbuf, dtype=jnp.int32), qpos])
    diff = qpos[:, None] - kpos[None, :]
    mask = (diff >= 0) & (diff <= WINDOW)
    qg = q.reshape(B, T, SW_KV_HEADS, SW_GROUP, SW_HD)
    s = jnp.einsum('btkgd,bskd->bkgts', qg, kc).astype(jnp.float32) * (SW_HD ** -0.5)
    s = jnp.where(mask[None, None, None], s, -jnp.inf)
    p = sink_probs(s, sinks).astype(v.dtype)
    o = jnp.einsum('bkgts,bskd->btkgd', p, vc).reshape(B, T, SW_HEADS * SW_HD)
    return o @ w_out, kc[:, -nbuf:], vc[:, -nbuf:]

def conv_ffn(xn, w_up, conv_w, conv_b, w_down, prev):
    u = xn @ w_up
    T = u.shape[1]
    up = jnp.concatenate([prev.astype(u.dtype), u], axis=1)
    c = conv_b
    for j in range(CONV_W):
        c = c + up[:, j:j + T] * conv_w[j]
    h = jax.nn.silu(c[..., :D_FF]) * c[..., D_FF:]
    return h @ w_down, up[:, -(CONV_W - 1):]

def ple_term(h, p, g, w_gate, w_proj):
    return jax.nn.sigmoid(rmsnorm(h, g) @ w_gate) * (p @ w_proj)

def setup_inputs(seed: int = 0) -> dict:
    key = jax.random.key(seed)
    ks = iter(jax.random.split(key, 32))

    def nrm(shape, scale=1.0):
        return jax.random.normal(next(ks), shape, jnp.float32) * scale

    nbuf = min(WINDOW, PAST_LEN)
    D = D_MODEL
    return {
        "x_prompt": nrm((BATCH, SEQ, D)),
        "x_sample": nrm((DEC_BATCH, DEC_SEQ, D)),
        "p_prompt": nrm((DEPTH, BATCH, SEQ, PLE_DIM)),
        "p_sample": nrm((DEPTH, DEC_BATCH, DEC_SEQ, PLE_DIM)),
        "state_mlstm_C": nrm((N_A, DEC_BATCH, ML_HEADS, ML_DK, ML_DV)),
        "state_mlstm_n": nrm((N_A, DEC_BATCH, ML_HEADS, ML_DK)),
        "state_mlstm_m": nrm((N_A, DEC_BATCH, ML_HEADS)),
        "cache_swa_k": nrm((N_B, DEC_BATCH, nbuf, SW_KV_HEADS, SW_HD)),
        "cache_swa_v": nrm((N_B, DEC_BATCH, nbuf, SW_KV_HEADS, SW_HD)),
        "state_conv": nrm((DEPTH, DEC_BATCH, CONV_W - 1, 2 * D_FF)),
        "g_pre_mix": 1.0 + nrm((DEPTH, D), 0.02),
        "g_post_mix": 1.0 + nrm((DEPTH, D), 0.02),
        "g_pre_ffn": 1.0 + nrm((DEPTH, D), 0.02),
        "g_post_ffn": 1.0 + nrm((DEPTH, D), 0.02),
        "g_ple": 1.0 + nrm((DEPTH, D), 0.02),
        "ml_w_in": nrm((N_A, D, ML_IN), D ** -0.5),
        "ml_b_gate": nrm((N_A, 2 * ML_HEADS), 0.1) + jnp.repeat(jnp.array([0.0, FORGET_BIAS], jnp.float32), ML_HEADS),
        "ml_w_out": nrm((N_A, D, D), D ** -0.5),
        "sw_w_in": nrm((N_B, D, SW_IN), D ** -0.5),
        "sw_sinks": nrm((N_B, SW_HEADS), 0.5),
        "sw_w_out": nrm((N_B, SW_HEADS * SW_HD, D), (SW_HEADS * SW_HD) ** -0.5),
        "ffn_w_up": nrm((DEPTH, D, 2 * D_FF), D ** -0.5),
        "ffn_conv_w": nrm((DEPTH, CONV_W, 2 * D_FF), CONV_W ** -0.5),
        "ffn_conv_b": nrm((DEPTH, 2 * D_FF), 0.02),
        "ffn_w_down": nrm((DEPTH, D_FF, D), D_FF ** -0.5),
        "ple_w_proj": nrm((DEPTH, PLE_DIM, D), PLE_DIM ** -0.5),
        "ple_w_gate": nrm((DEPTH, D, D), D ** -0.5),
    }

def reference(x_prompt, x_sample, p_prompt, p_sample, state_mlstm_C, state_mlstm_n, state_mlstm_m,
              cache_swa_k, cache_swa_v, state_conv, g_pre_mix, g_post_mix, g_pre_ffn, g_post_ffn, g_ple,
              ml_w_in, ml_b_gate, ml_w_out, sw_w_in, sw_sinks, sw_w_out,
              ffn_w_up, ffn_conv_w, ffn_conv_b, ffn_w_down, ple_w_proj, ple_w_gate):
    hp, hs = x_prompt, x_sample
    Bp = hp.shape[0]
    Cp, Np, Mp, Cs, Ns, Ms = [], [], [], [], [], []
    Kp, Vp, Ks, Vs = [], [], [], []
    convp, convs = [], []
    for i in range(DEPTH):
        j = i // N_MIXERS
        ap = rmsnorm(hp, g_pre_mix[i])
        a_s = rmsnorm(hs, g_pre_mix[i])
        if i % N_MIXERS == 0:
            zero = (jnp.zeros((Bp, ML_HEADS, ML_DK, ML_DV), jnp.float32),
                    jnp.zeros((Bp, ML_HEADS, ML_DK), jnp.float32),
                    jnp.zeros((Bp, ML_HEADS), jnp.float32))
            yp, (c1, n1, m1) = mlstm_mixer(ap, ml_w_in[j], ml_b_gate[j], ml_w_out[j], zero, ML_CHUNK)
            ys, (c2, n2, m2) = mlstm_mixer(a_s, ml_w_in[j], ml_b_gate[j], ml_w_out[j],
                                           (state_mlstm_C[j], state_mlstm_n[j], state_mlstm_m[j]), a_s.shape[1])
            Cp.append(c1); Np.append(n1); Mp.append(m1)
            Cs.append(c2); Ns.append(n2); Ms.append(m2)
        else:
            yp, k1, v1 = swa_prompt(ap, sw_w_in[j], sw_sinks[j], sw_w_out[j])
            ys, k2, v2 = swa_sample(a_s, sw_w_in[j], sw_sinks[j], sw_w_out[j], cache_swa_k[j], cache_swa_v[j])
            Kp.append(k1); Vp.append(v1); Ks.append(k2); Vs.append(v2)
        hp = hp + rmsnorm(yp, g_post_mix[i])
        hs = hs + rmsnorm(ys, g_post_mix[i])
        fp, cvp = conv_ffn(rmsnorm(hp, g_pre_ffn[i]), ffn_w_up[i], ffn_conv_w[i], ffn_conv_b[i], ffn_w_down[i],
                           jnp.zeros((Bp, CONV_W - 1, 2 * D_FF), hp.dtype))
        fs, cvs = conv_ffn(rmsnorm(hs, g_pre_ffn[i]), ffn_w_up[i], ffn_conv_w[i], ffn_conv_b[i], ffn_w_down[i],
                           state_conv[i])
        convp.append(cvp); convs.append(cvs)
        hp = hp + rmsnorm(fp, g_post_ffn[i])
        hs = hs + rmsnorm(fs, g_post_ffn[i])
        hp = hp + ple_term(hp, p_prompt[i], g_ple[i], ple_w_gate[i], ple_w_proj[i])
        hs = hs + ple_term(hs, p_sample[i], g_ple[i], ple_w_gate[i], ple_w_proj[i])
    return (hp, hs,
            jnp.stack(Cp), jnp.stack(Np), jnp.stack(Mp), jnp.stack(Kp), jnp.stack(Vp), jnp.stack(convp),
            jnp.stack(Cs), jnp.stack(Ns), jnp.stack(Ms), jnp.stack(Ks), jnp.stack(Vs), jnp.stack(convs))


_drawn_inputs = setup_inputs


def setup_inputs(seed=0):
    import zlib

    import numpy as np

    out = dict(_drawn_inputs(seed))
    spreads = {}
    factors = {'g_post_ffn': 3.377, 'g_ple': 200.0, 'sw_sinks': 8.0}
    for name, (base, spread) in spreads.items():
        noise = np.random.default_rng([zlib.crc32(name.encode()), seed]).standard_normal(out[name].shape)
        drawn = base * np.exp(spread * noise) if base else spread * noise
        out[name] = __import__('jax').numpy.asarray(drawn.astype(out[name].dtype))
    for name, factor in factors.items():
        out[name] = (out[name] * factor).astype(out[name].dtype)
    return out
```

```python
from contextlib import ExitStack

import concourse.bass as bass
from concourse import mybir

F32 = mybir.dt.float32
F32R = mybir.dt.float32r
ALU = mybir.AluOpType
ACT = mybir.ActivationFunctionType
AXX = mybir.AxisListType.X

P = 128
D = 1024
KT = D // P
SEQ, DEC = 512, 8
T = SEQ + DEC
HT = T // 2
NL = 2
EPS = 1e-6
NH, DV = 4, 256
DK_SCALE = float(P) ** -0.5
NB = SEQ // P
HD = 64
NKV, NG = 4, 4
NQ = NKV * NG
QK_SCALE = float(HD) ** -0.5
PAST, WINDOW, THETA = 2048, 128, 10000.0
FT = 22
UP = 2 * FT
DKH = FT // 2
EKT = 2
KMAX = DKH
CW = 3
NEG = -1.0e30
GATE2 = 32

STAGES = [("kv", 13, KT), ("qo", 12, KT), ("mout", KT, KT),
          ("up0", UP, KT), ("down0", 2 * KT, DKH), ("ple0", KT, KT + EKT),
          ("qkv", 12, KT), ("sout", KT, KT),
          ("up1", UP, KT), ("down1", 2 * KT, DKH), ("ple1", KT, KT + EKT)]
ORDER = [name for name, _, _ in STAGES]
COUNT = {name: n for name, n, _ in STAGES}
DEPTHK = {name: k for name, _, k in STAGES}
CHUNK0, TILE0 = {}, {}
for _i, _s in enumerate(ORDER):
    _p = ORDER[_i - 1] if _i else None
    CHUNK0[_s] = CHUNK0[_p] + COUNT[_p] if _i else 0
    TILE0[_s] = TILE0[_p] + (COUNT[_p] // 2 if _p[:4] == "down" else COUNT[_p]) if _i else 0

XSET = {s: KT * i for i, s in enumerate(["kv", "mout", "up0", "ple0", "qkv", "sout", "up1", "ple1"])}
NORM = {s: i for i, s in enumerate(["kv", "mout", "up0", "down0", "ple0", "qkv",
                                    "sout", "up1", "down1", "ple1"])}
ON_PE = {s: KT * i for i, s in enumerate(["kv", "up0", "ple0", "up1", "ple1"])}
ON_DVE = {s: (KT + 1) * i for i, s in enumerate(["mout", "down0", "qkv", "sout", "down1"])}
COPIED = {s: KT * i for i, s in enumerate(["mout", "down0", "sout", "down1"])}
G_PRE_MIX, G_POST_MIX, G_PRE_FFN, G_POST_FFN, G_PLE = range(5)

C_IDENT, C_ONES, C_CAUSAL, C_PERM, C_BAND = 0, P, 2 * P, 3 * P, 4 * P
C_SEL, C_HOT = 6 * P, 6 * P + NH * P
C_ALL = C_HOT + NH * NH


class Step:

    def __init__(self, i, k, by=2):
        self.i, self.k, self.by = i, k, by

    def __add__(self, n):
        return Step(self.i, self.k + n, self.by)

    def at(self, add=0):
        return self.by * self.i + (self.k + add)

    def pair(self, add=0):
        return self.by // 2 * self.i + (self.k // 2 + add)


class Chain:

    def __init__(self, eng, sem):
        self.eng, self.sem, self.n = eng, sem, 0

    def did(self, ins):
        ins.then_inc(self.sem, 1)
        self.n += 1

    def link(self, ins):
        self.did(ins)
        self.eng.wait_ge(self.sem, self.n)


def static(st):
    return isinstance(st.i, int)


def unroll(stage):
    return 4 if stage[:4] == "down" else 2


def windows(eng, stage, peel, at_window):
    n, by = COUNT[stage], unroll(stage)
    loops = (n - 2 - peel) // by
    peel = n - 2 - by * loops
    for w in range(1, peel + 1):
        at_window(Step(0, w, by))
    with eng.Fori(0, loops) as i:
        for j in range(by):
            at_window(Step(i, peel + 1 + j, by))
    for w in (n - 1, n):
        at_window(Step(0, w, by))


def build(nc, g):
    with ExitStack() as ctx:
        def at(name, shape, offset, dt=F32):
            return nc.alloc_sbuf_tensor_at(name, shape, dt, offset=offset)

        def size(shape):
            n = 4
            for s in shape[1:]:
                n *= s
            return (n + 31) // 32 * 32

        class Region:
            def __init__(self, start):
                self.top = start

            def __call__(self, name, shape, dt=F32):
                t = at(name, shape, self.top, dt)
                self.top += size(shape)
                assert self.top <= nc.sbuf_usable_end, (name, self.top - nc.sbuf_usable_end)
                return t

        def sem(name):
            return ctx.enter_context(nc.semaphore(name))

        def psum(name, shape):
            return ctx.enter_context(nc.psum_tensor(name, shape, F32))

        sb = Region((nc.sbuf_base + 31) // 32 * 32)
        h = sb("h", [P, KT, T])
        xH = sb("xH", [P, KT, T], F32R)
        xL_at = sb.top
        xL = sb("xL", [P, KT, T], F32R)
        raw = sb("raw", [P, 2, KMAX * P])
        wH = sb("wH", [P, 2, KMAX * P], F32R)
        wL = sb("wL", [P, 2, KMAX * P], F32R)
        u = sb("u", [P, 2, T + 2])
        cg = sb("cg", [P, T])
        cv = sb("cv", [P, T])
        sq = sb("sq", [P, 2, T])
        acc = sb("acc", [P, T])
        rstd = sb("rstd", [P, T])
        convw = sb("convw", [P, UP, 4])
        prev = sb("prev", [P, UP, CW - 1, DEC])
        newrows = sb("newrows", [P, UP, 2 + DEC])
        gains = sb("gains", [P, NL, 5, KT])
        const = sb("const", [P, C_ALL])
        eps = sb("eps", [P, 1])
        touch = sb("touch", [P, 1])
        taps = sb("taps", [P, 2, 4])
        ident = const[:, C_IDENT:C_IDENT + P]
        ones = const[:, C_ONES:C_ONES + P]
        causal = const[:, C_CAUSAL:C_CAUSAL + P]
        perm = const[:, C_PERM:C_PERM + P]
        band = const[:, C_BAND:C_BAND + 2 * P]
        sel = const[0:NH, C_SEL:C_SEL + NH * P].rearrange("k (h m) -> k h m", h=NH)
        hot = const[:, C_HOT:C_HOT + NH * NH].rearrange("p (h m) -> p h m", h=NH)
        arena = sb.top

        y_down = at("y_down", [P, KT, T], xL_at)
        ff = Region(arena)
        hidH = ff("hidH", [P, FT, T], F32R)
        hidL = ff("hidL", [P, FT, T], F32R)
        em = Region(arena)
        pxH = em("pxH", [P, KT, T], F32R)
        pxL = em("pxL", [P, KT, T], F32R)
        pin = em("pin", [P, EKT, T])
        pH = em("pH", [P, EKT, T], F32R)
        pL = em("pL", [P, EKT, T], F32R)
        ml = Region(arena)
        kvq = ml("kvq", [P, 4 * NH, T])
        y_ml = at("y_ml", [P, KT, T], ml.top)
        ktok = ml("ktok", [P, NB, NH, P])
        vtok = ml("vtok", [P, NB, NH, DV])
        ktoks = ml("ktoks", [DEC, NH, P])
        vtoks = ml("vtoks", [DEC, NH, DV])
        vmask = ml("vmask", [DEC, 2, NH, DV])
        prob = ml("prob", [P, 2, 1280])
        cring = ml("cring", [P, 2, NH, DV])
        cfin = ml("cfin", [P, NH, DV + 1])
        kw = cv[:, 0:NB * P].rearrange("p (b d) -> p b d", b=NB)
        brow = ml("brow", [NH, SEQ])
        mrow = ml("mrow", [NH, SEQ])
        erow = u[0:NH, 1, 0:SEQ]
        gbias = ml("gbias", [P, 1])
        minit = ml("minit", [NH, DEC])
        mout = ml("mout", [NH, 1 + DEC])
        srow = ml("srow", [NH, 3, DEC])
        acol = ml("acol", [P, NB, NH])
        wcol = ml("wcol", [P, NB, NH])
        wscol = ml("wscol", [DEC, NH])
        sbc = ml("sbc", [P, NH, 3, DEC])
        nst = ml("nst", [P, NH, DEC])
        ntmp = ml("ntmp", [P, 2, NH, DEC])
        rs = ml("rs", [P, NH, DEC])
        stmp = ml("stmp", [P, NH, 2, DEC])
        sw = Region(arena)
        y_sw = at("y_sw", [P, KT, T], sw.top)
        qk = sw("qk", [P, 2 + KT, T])
        vs = sw("vs", [P, 2, T])
        vst = sw("vst", [P, NB, NKV * HD])
        vnew = sw("vnew", [DEC, NKV * HD])
        att = sw("att", [P, KT, T])
        sw.top = max(sw.top, em.top)
        kc = sw("kc", [P, DEC, 2, WINDOW + 1])
        vc = sw("vc", [P, DEC, NKV * HD])
        cos_t = sw("cos_t", [P, T])
        sin_t = sw("sin_t", [P, T])
        qpad = sw("qpad", [P, DEC * 2, P])
        soft = sw("soft", [P, 2, 4, 2 * P])
        softT = sw("softT", [P, 2, 4, 2 * P])
        sinks = sw("sinks", [P, NQ + 1])
        identR = sw("identR", [P, P], F32R)
        bandR = sw("bandR", [P, 2 * P], F32R)
        sm = sw("sm", [P, 2, 4, 4])
        sp = sw("sp", [P, WINDOW + 1])
        spd = sw("spd", [P, P])
        spT = sw("spT", [P, 2 * P])
        sst = sw("sst", [P, 8])

        tile = [psum(f"tile{k}", [P, 2, 512]) for k in range(2)]
        sums = psum("sums", [P, 2, 512])
        side = psum("side", [P, 2, 512])

        s_const, s_x, s_gain, s_gb = sem("const_in"), sem("x_in"), sem("gain_in"), sem("gate_bias_in")
        s_raw = [sem(f"weights_in{k}") for k in range(2)]
        s_high, s_low = sem("weights_high"), sem("weights_low")
        s_mm, s_read = sem("chunk_done"), sem("tile_read")
        s_eps, s_h = sem("eps_set"), sem("embedding_added")
        s_xh, s_xr, s_sq, s_squ = sem("x_high"), sem("x_ready"), sem("squared"), sem("squares_summed")
        s_acc, s_ss, s_root, s_rstd = sem("acc_done"), sem("sum_ready"), sem("root_ready"), sem("rstd_ready")
        s_yc, s_dve, s_act = sem("y_copied"), sem("dve_step"), sem("act_step")
        s_cw, s_pv0, s_ca, s_cc = sem("conv_in"), sem("conv_past"), sem("conv_first"), sem("conv_done")
        s_silu, s_gated, s_hh, s_hid = sem("silu_done"), sem("gated"), sem("hid_high"), sem("hid_ready")
        s_c1, s_update, s_added = sem("conv_second"), sem("update_ready"), sem("update_added")
        s_pad, s_p, s_ph, s_pr = sem("pad_zero"), sem("p_in"), sem("p_high"), sem("p_ready")
        s_sig, s_side = sem("sigmoid_done"), sem("side_read")
        s_pleh, s_psq = sem("ple_h"), sem("ple_square")
        s_out = sem("stored")
        s_st, s_nabs, s_ln, s_rows, s_rexp = (sem("state_in"), sem("gate_abs"), sem("gate_ln"),
                                              sem("rows_ready"), sem("rows_exp"))
        s_cols, s_dml, s_wcol, s_bcr = sem("cols_ready"), sem("col_shift"), sem("wcol_ready"), sem("cols_read")
        s_turn, s_trd, s_tra, s_tsr = sem("turned"), sem("turn_read_dve"), sem("turn_read_act"), sem("turn_samples")
        s_mb, s_diag, s_expd, s_score, s_prob = (sem("m_spread"), sem("diag_ready"), sem("decay_ready"),
                                                 sem("scores_ready"), sem("prob_ready"))
        s_num, s_nr, s_kw, s_cf, s_cfr = (sem("num_ready"), sem("num_read"), sem("kw_ready"),
                                          sem("cfin_ready"), sem("cfin_read"))
        s_sigo, s_rrow, s_rbc, s_afin = sem("o_sigmoid"), sem("rrow_ready"), sem("r_spread"), sem("mix_ready")
        s_cin = [sem(f"c_in{k}") for k in range(2)]
        s_cst = [sem(f"c_stored{k}") for k in range(2)]
        s_vm, s_outer, s_cnew, s_snum, s_qns, s_prod = (sem("vmask_ready"), sem("outer_done"), sem("c_new"),
                                                       sem("sample_num"), sem("sample_qn"), sem("sample_prod"))
        s_swc, s_qz, s_rot, s_rotr, s_swk, s_rope = (sem("window_in"), sem("qpad_zero"), sem("rotated"),
                                                    sem("rot_read"), sem("consts_rounded"), sem("rope_done"))
        s_vt, s_vtr, s_qp, s_sps, s_sz, s_se = (sem("v_turned"), sem("v_turn_read"), sem("qpad_ready"),
                                               sem("sample_scores"), sem("sample_shift"), sem("sample_exp"))
        s_spn, s_spt, s_sptr, s_spv, s_satt = (sem("sample_soft"), sem("sample_turned"), sem("sample_turn_read"),
                                              sem("sample_pv"), sem("sample_att"))
        s_z, s_soft, s_norm, s_tu, s_tua, s_tud, s_pv, s_or = (
            sem("shift_ready"), sem("soft_exp"), sem("soft_ready"), sem("soft_turned"),
            sem("soft_read_act"), sem("soft_read_dve"), sem("pv_done"), sem("att_read"))

        STORED_L0 = 10

        block = ctx.enter_context(nc.Block())

        def slot(stage, k):
            return (CHUNK0[stage] + k) % 2

        def pslot(stage, k):
            return (TILE0[stage] + k) % 2

        def halves(ap):
            return ap.rearrange("p (q t) -> p q t", q=2)

        def following(stage):
            i = ORDER.index(stage) + 1
            return ORDER[i] if i < len(ORDER) else None

        @block.sync
        def _(sp):
            sp.dma_start(h[:, 0:2, :], g.x[:, 0:2, :]).then_inc(s_x, 16)
            sp.dma_start(gains[:], g.gains).then_inc(s_gain, 16)
            sp.dma_start(const[:], g.const).then_inc(s_const, 16)

            def load(stage, st):
                k, c0, w = slot(stage, st.k), CHUNK0[stage], g.weights[stage]
                if c0 + st.k >= 2:
                    sp.wait_ge(s_low, st.at(c0 - 1))
                sp.dma_start(raw[:, k, 0:DEPTHK[stage] * P],
                             w[bass.ds(st.at(), 1), :, :].rearrange("o p f -> p (o f)")
                             ).then_inc(s_raw[k], 16)

            for stage in ORDER:
                first = 2 + COUNT[stage] % 2
                for c in range(first):
                    load(stage, Step(0, c))
                    if stage == "kv" and c == 0:
                        sp.dma_start(h[:, 2:KT, :], g.x[:, 2:KT, :]).then_inc(s_x, 16)
                with sp.Fori(0, (COUNT[stage] - first) // 2) as i:
                    for j in range(2):
                        load(stage, Step(i, first + j))

        update = (cv, rstd)

        @block.gpsimd
        def _(pool):
            def add_update(u0):
                for k in range(KT):
                    pool.wait_ge(s_update, u0 + k + 1)
                    nc.gpsimd.tensor_tensor(h[:, k, :], h[:, k, :], update[k % 2][:], ALU.add).then_inc(s_added, 1)

            nc.gpsimd.memset(eps[:], EPS).then_inc(s_eps, 1)
            pool.dma_start(gbias[0:GATE2 + NH, :], g.gate_bias).then_inc(s_gb, 16)
            pool.dma_start(minit[:], g.m_in).then_inc(s_st, 16)
            pool.dma_start(nst[:], g.n_in).then_inc(s_st, 16)
            for b in range(2):
                pool.dma_start(cring[:, b], g.c_in[b]).then_inc(s_cin[b], 16)
            pool.dma_start(g.conv_old, g.conv_prev[:, :, :, 1, :]).then_inc(s_out, 16)
            pool.dma_start(g.v_s[0:WINDOW - 1], g.vc_in[1:WINDOW]).then_inc(s_out, 16)
            stored = 2

            for b in range(DEC):
                pool.wait_ge(s_cnew, b + 1)
                pool.dma_start(g.c_s[b], cring[:, b % 2]).then_inc(s_cst[b % 2], 16)
                if b + 2 < DEC:
                    pool.wait_ge(s_cst[b % 2], 16 * (b // 2 + 1))
                    pool.wait_ge(s_snum, b + 1)
                    pool.dma_start(cring[:, b % 2], g.c_in[b + 2]).then_inc(s_cin[b % 2], 16)
            pool.wait_ge(s_prod, 1)
            pool.dma_start(g.n_s, nst[:]).then_inc(s_out, 16)
            pool.wait_ge(s_rows, 1)
            pool.dma_start(g.m_all, mout[:]).then_inc(s_out, 16)
            pool.wait_ge(s_cfr, NH)
            pool.dma_start(g.c_p, cfin[:]).then_inc(s_out, 16)
            stored += 3
            for b in range(2):
                pool.wait_ge(s_cst[b], 16 * DEC // 2)

            pool.wait_ge(s_out, 16 * stored)

            for layer in range(NL):
                up, down, ple = f"up{layer}", f"down{layer}", f"ple{layer}"
                if layer:
                    pool.wait_ge(s_hid, FT)
                    pool.wait_ge(s_out, 16 * stored)
                pool.dma_start(convw[:], g.convw[layer]).then_inc(s_cw, 16)
                pool.dma_start(prev[:], g.conv_prev[layer]).then_inc(s_cw, 16)
                pool.wait_ge(s_afin if layer == 0 else s_rope, NH + 1 if layer == 0 else 2 + KT)
                nc.gpsimd.memset(u[:, :, 0:2], 0.0).then_inc(s_pad, 1)
                add_update(2 * KT * layer)
                pool.wait_ge(s_hid, FT * (layer + 1))
                pool.dma_start(g.newrows[layer], newrows[:]).then_inc(s_out, 16)
                stored += 1
                pool.wait_ge(s_mm, CHUNK0[ple])
                pool.dma_start(pin[:], g.p[layer]).then_inc(s_p, 16)
                add_update(2 * KT * layer + KT)
                if layer == 0:
                    nc.gpsimd.memset(qpad[:], 0.0).then_inc(s_qz, 1)
                    for dst, src in ((kc[:, :, :, 0:WINDOW], g.kc_in), (vc[:], g.vc_in), (cos_t[:], g.cos_t),
                                     (sin_t[:], g.sin_t), (sinks[:], g.sinks)):
                        pool.dma_start(dst, src).then_inc(s_swc, 16)
                    pool.wait_ge(s_rope, 2 + KT)
                    pool.dma_start(g.k_p, qk[:, 0:2, SEQ - WINDOW:SEQ]).then_inc(s_out, 16)
                    pool.dma_start(g.v_p, vs[:, :, SEQ - WINDOW:SEQ]).then_inc(s_out, 16)
                    pool.wait_ge(s_qp, 1)
                    pool.dma_start(g.k_s, kc[:, :, :, 1:WINDOW + 1]).then_inc(s_out, 16)
                    pool.wait_ge(s_vtr, 3)
                    pool.dma_start(g.v_s[WINDOW - 1], vnew[:]).then_inc(s_out, 16)
                    stored += 4
                    assert stored == STORED_L0
            for k in range(0, KT, 4):
                pool.wait_ge(s_h, KT + k + 4)
                pool.dma_start(g.y[:, k:k + 4, :], h[:, k:k + 4, :]).then_inc(s_out, 16)
                stored += 1
            pool.wait_ge(s_out, 16 * stored)

        def landed(stage, st):
            return 16 * (st.by // 2 * st.i + ((CHUNK0[stage] + st.k) // 2 + 1))

        def turned_to(i):
            if i < NH:
                return ktok[:, :, i, :], ktoks[:, i, :]
            n, half = divmod(i - NH, 2)
            return vtok[:, :, n, half * P:half * P + P], vtoks[:, n, half * P:half * P + P]

        def o_tile(k):
            return kvq[:, NH + k, :]

        @block.scalar
        def _(act):
            chain = Chain(act, s_act)

            def high(stage, st):
                k, c0, n = slot(stage, st.k), CHUNK0[stage], DEPTHK[stage] * P
                act.wait_ge(s_raw[k], landed(stage, st))
                if c0 + st.k >= 2:
                    act.wait_ge(s_mm, st.at(c0 - 1))
                nc.scalar.activation(wH[:, k, 0:n], raw[:, k, 0:n], ACT.Copy).then_inc(s_high, 1)

            def stream(stage, peel, read):
                def at_window(st):
                    if st.k + 1 < COUNT[stage] or not static(st):
                        high(stage, st + 1)
                    elif st.k + 1 == COUNT[stage] and following(stage):
                        high(following(stage), Step(0, 0))
                    read(st + -1)
                windows(act, stage, peel, at_window)

            def second(stage):
                high(stage, Step(0, 1))

            def root(stage, dst):
                if stage in ON_PE:
                    act.wait_ge(s_squ, ON_PE[stage] + KT)
                else:
                    act.wait_ge(s_ss, sorted(ON_DVE.values()).index(ON_DVE[stage]) + 1)
                act.wait_ge(s_eps, 1)
                nc.scalar.activation(halves(dst[:]), sums[:, :, 0:HT], ACT.Sqrt, bias=eps[:, 0:1],
                                     scale=1.0 / D).then_inc(s_root, 1)

            def inputs(stage, dst, layer, norm, added):
                for k in range(KT):
                    if added is not None:
                        act.wait_ge(s_added, added + k + 1)
                    act.wait_ge(s_gain, 16)
                    nc.scalar.activation(dst[:, k, :], h[:, k, :], ACT.Copy,
                                         scale=gains[:, layer, norm, k:k + 1]).then_inc(s_xh, 1)
                    if ON_PE[stage] + k >= 2:
                        act.wait_ge(s_squ, ON_PE[stage] + k - 1)
                    nc.scalar.activation(sq[:, k % 2, :], h[:, k, :], ACT.Square).then_inc(s_sq, 1)

            def squares(stage, by):
                def read(st):
                    if by == 2 and st.k % 2 == 0:
                        return
                    o, k = (st.pair, st.k // 2) if by == 2 else (st.at, st.k)
                    act.wait_ge(s_yc, o(COPIED[stage] + 1))
                    if ON_DVE[stage] + k > 0:
                        act.wait_ge(s_acc, o(ON_DVE[stage]))
                    nc.scalar.activation(halves(sq[:, k % 2, :]), tile[pslot(stage, k)][:, :, 0:HT],
                                         ACT.Square).then_inc(s_read, 1)
                return read

            act.wait_ge(s_x, 32)
            high("kv", Step(0, 0))
            inputs("kv", xH, 0, G_PRE_MIX, None)
            second("kv")
            root("kv", rstd)

            def gates(st):
                if static(st) and st.k == 0:
                    act.wait_ge(s_nabs, 1)
                    chain.link(nc.scalar.activation(u[0:NH, 1, 0:T], u[0:NH, 1, 0:T], ACT.Exp))
                    nc.scalar.activation(u[0:NH, 1, 0:T], u[0:NH, 1, 0:T], ACT.Ln, bias=1.0).then_inc(s_ln, 1)

            stream("kv", 1, gates)
            second("qo")
            act.wait_ge(s_rows, 1)
            nc.scalar.activation(erow, brow[:], ACT.Exp, scale=-1.0).then_inc(s_rexp, 1)
            nc.scalar.activation(srow[:], srow[:], ACT.Exp).then_inc(s_rexp, 1)
            for i in range(1, 3 * NH, 2):
                act.wait_ge(s_turn, i + 1)
                nc.scalar.activation(turned_to(i)[0], side[:, 1, :].rearrange("p (b c) -> p b c", b=NB),
                                     ACT.Copy).then_inc(s_tra, 1)
            act.wait_ge(s_dml, 1)
            nc.scalar.activation(wcol[:], wcol[:], ACT.Exp).then_inc(s_wcol, 1)
            stream("qo", 4, lambda st: None)
            second("mout")
            act.wait_ge(s_read, TILE0["mout"])
            for k in range(0, KT, 4):
                nc.scalar.activation(kvq[:, NH + k:NH + k + 4, :], kvq[:, NH + k:NH + k + 4, :],
                                     ACT.Sigmoid).then_inc(s_sigo, 1)
            for n in range(NH):
                act.wait_ge(s_mb, n + 1)
                act.wait_ge(s_diag, n + 1)
                if n >= 2:
                    act.wait_ge(s_num, n - 1)
                at0 = 0
                for j in range(NB):
                    bias = acol[:, j, n:n + 1]
                    last = nc.scalar.activation(prob[:, n % 2, at0:at0 + P], cg[:, j * P:j * P + P],
                                                ACT.Exp, bias=bias)
                    if j < NB - 1:
                        nc.scalar.activation(prob[:, n % 2, at0 + P:at0 + SEQ - j * P],
                                             sums[:, 0, (j + 1) * P:SEQ], ACT.Exp, bias=bias, scale=-1.0)
                    at0 += SEQ - j * P
                last.then_inc(s_expd, 1)
            for k in range(KT):
                act.wait_ge(s_afin, k // 2 + 2)
                nc.scalar.activation(xH[:, k, :], o_tile(k), ACT.Copy).then_inc(s_xh, 1)

            def feed_forward(layer, mixer, sqs):
                up, down, ple = f"up{layer}", f"down{layer}", f"ple{layer}"
                stream(mixer, 2, squares(mixer, 1))
                second(up)
                root(mixer, cg)
                inputs(up, xH, layer, G_PRE_FFN, 2 * KT * layer)
                root(up, rstd)

                def hid_high(p):
                    act.wait_ge(s_gated, p(FT * layer + 1))
                    nc.scalar.activation(touch[:], eps[:], ACT.Copy)
                    nc.scalar.activation(hidH[:, bass.ds(p(), 1), :].rearrange("p o t -> p (o t)"), cv[:],
                                         ACT.Copy).then_inc(s_hh, 1)

                def silu_and_tap(st):
                    r, c = st.k % 2, (cg, cv)[st.k % 2]
                    if r:
                        act.wait_ge(s_cc, st.at(UP * layer))
                        nc.scalar.activation(cg[:], cg[:], ACT.Silu).then_inc(s_silu, 1)
                        if not static(st) or st.k > 1:
                            act.wait_ge(s_hid, st.pair(FT * layer))
                    elif not static(st) or st.k:
                        hid_high((st + -1).pair)
                    act.wait_ge(s_read, st.at(TILE0[up] + 1))
                    nc.scalar.activation(c[:], u[:, r, 2:], ACT.Identity, bias=taps[:, r, 3:4],
                                         scale=taps[:, r, 2:3]).then_inc(s_ca, 1)

                stream(up, 2, silu_and_tap)
                hid_high(Step(0, UP - 1).pair)
                second(down)
                stream(down, 2, squares(down, 2))
                second(ple)
                root(down, cg)
                inputs(ple, pxH, layer, G_PLE, 2 * KT * layer + KT)
                act.wait_ge(s_p, 16 * (layer + 1))
                nc.scalar.activation(pH[:], pin[:], ACT.Copy).then_inc(s_ph, 1)
                root(ple, rstd)

                def sigmoid(st):
                    act.wait_ge(s_read, st.at(TILE0[ple] + 1))
                    nc.scalar.activation(cg[:], cg[:], ACT.Sigmoid).then_inc(s_sig, 1)

                stream(ple, 2, sigmoid)

            feed_forward(0, "mout", None)

            second("qkv")
            root("qkv", rstd)
            act.wait_ge(s_swc, 16 * 5)
            act.wait_ge(s_const, 16)
            nc.scalar.activation(identR[:], ident, ACT.Copy).then_inc(s_swk, 1)
            nc.scalar.activation(bandR[:], band, ACT.Copy).then_inc(s_swk, 1)
            stream("qkv", 4, lambda st: None)
            second("sout")
            def exps(gi):
                w0 = P if gi < 4 else 0
                act.wait_ge(s_z, gi + 1)
                if gi >= 2:
                    act.wait_ge(s_tu, gi - 1)
                k = gi % 2
                for c in range(4):
                    nc.scalar.activation(soft[:, k, c, w0:], tile[k][:, c // 2, (c % 2) * 2 * P + w0:(c % 2 + 1) * 2 * P],
                                         ACT.Exp, bias=sm[:, k, 0, c:c + 1], scale=QK_SCALE,
                                         accum_out=sm[:, k, 3, c:c + 1])
                nc.scalar.activation(sm[:, k, 2, :], sm[:, k, 1, :], ACT.Exp).then_inc(s_soft, 1)

            def turn_read(gi):
                act.wait_ge(s_tu, gi + 1)
                if gi >= 2:
                    act.wait_ge(s_pv, gi - 1)
                lo = 1 if gi < 4 else 0
                nc.scalar.activation(softT[:, gi % 2, 0:2, lo * P:].rearrange("p c (b t) -> p c b t", t=P),
                                     side[:, 0, :].rearrange("p (c b t) -> p c b t", c=2, b=2)[:, :, lo:, :],
                                     ACT.Copy).then_inc(s_tua, 1)

            def att_read(gi):
                n, gp = divmod(gi, 4)
                act.wait_ge(s_pv, gi + 1)
                nc.scalar.activation(att[:, 2 * gp:2 * gp + 2, n * P:n * P + P],
                                     sums[:, gi % 2, 0:2 * P].rearrange("p (c t) -> p c t", c=2),
                                     ACT.Copy).then_inc(s_or, 1)

            groups = 4 * NB
            def x_high(gp):
                act.wait_ge(s_or, groups - 4 + gp + 1)
                act.wait_ge(s_satt, 1)
                for k in (2 * gp, 2 * gp + 1):
                    nc.scalar.activation(xH[:, k, :], att[:, k, :], ACT.Copy).then_inc(s_xh, 1)

            exps(0)
            for gi in range(groups):
                if gi + 1 < groups:
                    exps(gi + 1)
                turn_read(gi)
                if gi >= 1:
                    att_read(gi - 1)
                if gi == 0:
                    act.wait_ge(s_sz, 1)
                    nc.scalar.activation(sp[:], sums[:, 0, 2 * P:3 * P + 1], ACT.Exp, bias=sst[:, 1:2],
                                         scale=QK_SCALE, accum_out=sst[:, 3:4]).then_inc(s_se, 1)
                    nc.scalar.activation(sst[:, 4:5], sst[:, 2:3], ACT.Exp).then_inc(s_se, 1)
                if gi >= groups - 3:
                    x_high(gi - (groups - 3))
            att_read(groups - 1)
            x_high(3)
            feed_forward(1, "sout", None)

        @block.tensor
        def _(pe):
            def product(stage, st, x, k, out, first, last):
                s = slot(stage, st.k)
                w = slice(k * P, k * P + P)
                for n, (wt, xt) in enumerate(((wH, x[0]), (wH, x[1]), (wL, x[0]))):
                    for q in range(2):
                        mm = nc.tensor.matmul(out[:, q, 0:HT], wt[:, s, w], xt[:, k + x[2], q * HT:(q + 1) * HT],
                                              start=first and n == 0, stop=last and n == 2)
                return mm

            def chunk(stage, st, x, fresh=False, direct=False):
                pe.wait_ge(s_low, st.at(CHUNK0[stage] + 1))
                down = stage[:4] == "down"
                o, k0 = (st.pair, st.k // 2) if down else (st.at, st.k)
                if TILE0[stage] + k0 >= 2 and not (down and st.k % 2):
                    pe.wait_ge(s_read, o(TILE0[stage] - 1))
                out = tile[pslot(stage, k0)]
                part = st.k % 2 if down else 0
                xs = (x[0], x[1], part * DKH) if down else (x[0], x[1], 0)
                if direct and NORM[stage]:
                    pe.wait_ge(s_root, NORM[stage])
                n = DKH if down else KT
                for k in range(n):
                    if fresh:
                        pe.wait_ge(s_xr, XSET[stage] + k + 1)
                    mm = product(stage, st, xs, k, out, k == 0 and part == 0, k == n - 1 and (not down or part == 1))
                    if direct:
                        pe.wait_ge(s_sq, ON_PE[stage] + k + 1)
                        for q in range(2):
                            ms = nc.tensor.matmul(sums[:, q, 0:HT], ones, sq[:, k % 2, q * HT:(q + 1) * HT],
                                                  start=(k == 0), stop=(k == KT - 1))
                        ms.then_inc(s_squ, 1)
                if stage[:3] == "ple":
                    done = KT * int(stage[3]) + st.k
                    if done or not static(st):
                        pe.wait_ge(s_side, st.at(KT * int(stage[3])))
                    if static(st) and st.k == 0:
                        pe.wait_ge(s_pr, int(stage[3]) + 1)
                    s = slot(stage, st.k)
                    for k in range(EKT):
                        w = slice((KT + k) * P, (KT + k + 1) * P)
                        for n, (wt, xt) in enumerate(((wH, pH), (wH, pL), (wL, pH))):
                            for q in range(2):
                                mm = nc.tensor.matmul(side[:, q, 0:HT], wt[:, s, w], xt[:, k, q * HT:(q + 1) * HT],
                                                      start=(k == 0 and n == 0), stop=(k == EKT - 1 and n == 2))
                mm.then_inc(s_mm, 1)

            def chunks(stage, x, fresh=True, direct=False, extra=None, peel=2):
                by = unroll(stage)
                n = COUNT[stage]
                peel += (n - peel) % by
                for c in range(peel):
                    if stage[:4] == "down":
                        pe.wait_ge(s_hid, FT * int(stage[4]) + (DKH if c == 0 else FT))
                    chunk(stage, Step(0, c, by), x, fresh and c == 0, direct and c == 0)
                    if extra:
                        extra(Step(0, c, by))
                with pe.Fori(0, (n - peel) // by) as i:
                    for j in range(by):
                        chunk(stage, Step(i, peel + j, by), x)
                        if extra:
                            extra(Step(i, peel + j, by))

            def sum_acc(stage):
                pe.wait_ge(s_acc, ON_DVE[stage] + KT + 1)
                pe.wait_ge(s_root, NORM[stage])
                for q in range(2):
                    mm = nc.tensor.matmul(sums[:, q, 0:HT], ones, acc[:, q * HT:(q + 1) * HT], start=True, stop=True)
                mm.then_inc(s_ss, 1)

            pe.wait_ge(s_const, 16)
            X = (xH, xL)
            chunks("kv", X, direct=True, peel=3)

            for i in range(3 * NH):
                if i == 0:
                    pe.wait_ge(s_read, TILE0["qo"])
                    pe.wait_ge(s_root, 1)
                if i >= 2:
                    pe.wait_ge(s_trd if i % 2 == 0 else s_tra, i // 2)
                if i >= 4 and i % 4 == 0:
                    pe.wait_ge(s_tsr, i // 4)
                nc.tensor.transpose(sums[0:DEC, 0, (i % 4) * P:(i % 4 + 1) * P], kvq[:, i, SEQ:T], ident)
                for b in range(NB):
                    mm = nc.tensor.transpose(side[:, i % 2, b * P:b * P + P], kvq[:, i, b * P:b * P + P], ident)
                mm.then_inc(s_turn, 1)
            pe.wait_ge(s_rexp, 2)
            for b in range(NB):
                nc.tensor.matmul(sums[:, 1, NH * b:NH * b + NH], cv[0:NH, b * P:b * P + P], ident[0:NH, 0:NH],
                                 start=True, stop=True)
            nc.tensor.matmul(sums[0:DEC, 1, 16:16 + NH], srow[:, 1, :], ident[0:NH, 0:NH], start=True, stop=True)
            for n in range(NH):
                nc.tensor.matmul(sums[:, 1, 32 + 24 * n:56 + 24 * n], sel[:, n, :],
                                 srow[:].rearrange("k a b -> k (a b)"), start=True, stop=True)
                mm = nc.tensor.matmul(sums[:, 1, 128 + n:129 + n], sel[:, n, :], mrow[:, SEQ - 1:SEQ],
                                      start=True, stop=True)
            mm.then_inc(s_cols, 1)

            def memory_query(b):
                pe.wait_ge(s_cnew, b.at(1))
                for n in range(NH):
                    for half in range(2):
                        mm = nc.tensor.matmul(sums[:, 1, bass.ds(b.at((2 * n + half) * DEC), 1)],
                                              cring[:, b.k % 2, n, half * P:half * P + P],
                                              kvq[:, 3 * NH + n, bass.ds(b.at(SEQ), 1)], start=True, stop=True)
                mm.then_inc(s_snum, 1)

            def sample_products(st):
                b = st + -NH
                if static(b) and b.k < 0:
                    return
                first = static(b) and b.k == 0
                if first:
                    pe.wait_ge(s_tra, 3 * NH // 2)
                else:
                    pe.wait_ge(s_cnew, b.at())
                pe.wait_ge(s_vm, b.at(1))
                for n in range(NH):
                    mm = nc.tensor.matmul(side[:, n // 2, (n % 2) * DV:(n % 2 + 1) * DV], ktoks[:, n, :],
                                          vmask[:, b.k % 2, n, :], start=True, stop=True)
                mm.then_inc(s_outer, 1)
                if not first:
                    memory_query(b + -1)

            chunks("qo", X, fresh=False, extra=sample_products, peel=NH + 2)
            memory_query(Step(0, DEC - 1))
            pe.wait_ge(s_read, TILE0["mout"])
            pe.wait_ge(s_prod, 1)
            nc.tensor.matmul(sums[:, 1, P:P + NH * DEC], ones, ntmp[:, 0].rearrange("p n b -> p (n b)"),
                             start=True, stop=True).then_inc(s_qns, 1)

            st_at = [(0, 0), (0, 512), (1, 0), (1, 256)]

            def spread_scores(n):
                if n >= 1:
                    pe.wait_ge(s_expd, n)
                nc.tensor.matmul(sums[:, 0, :], sel[:, n, :], mrow[:], start=True, stop=True).then_inc(s_mb, 1)
                if n >= 1:
                    pe.wait_ge(s_prob, n)
                for j in range(NB):
                    b, c = st_at[j]
                    w = SEQ - j * P
                    out = tile[b][:].rearrange("p q t -> p (q t)")[:, c:c + w]
                    mm = nc.tensor.matmul(out, kvq[:, n, j * P:j * P + P], kvq[:, 3 * NH + n, j * P:SEQ],
                                          start=True, stop=True)
                mm.then_inc(s_score, 1)

            def values(n):
                pe.wait_ge(s_prob, n + 1)
                if n >= 1:
                    pe.wait_ge(s_nr, n)
                else:
                    pe.wait_ge(s_afin, 1)
                at0 = 0
                for j in range(NB):
                    w = SEQ - j * P
                    pj = prob[:, n % 2, at0:at0 + w]
                    for half in range(2):
                        nc.tensor.matmul(side[:, half, j * P:SEQ], vtok[:, j, n, half * P:half * P + P], pj,
                                         start=(j == 0), stop=(j == NB - 1), skip_group_check=True)
                    mm = nc.tensor.matmul(tile[1][0:NH, 1, j * P:SEQ], hot[:, n, :], pj, start=(n == 0 and j == 0),
                                          stop=(n == NH - 1 and j == NB - 1), skip_group_check=True)
                    at0 += w
                mm.then_inc(s_num, 1)
                pe.wait_ge(s_kw, n + 1)
                if n >= 1:
                    pe.wait_ge(s_cfr, n)
                for j in range(NB):
                    nc.tensor.matmul(sums[:, 1, 0:DV], kw[:, j, :], vtok[:, j, n, :], start=(j == 0),
                                     stop=(j == NB - 1), skip_group_check=True)
                for j in range(NB):
                    mm = nc.tensor.matmul(sums[:, 1, DV:DV + 1], kw[:, j, :], ones[:, 0:1], start=False,
                                          stop=(j == NB - 1), skip_group_check=True)
                mm.then_inc(s_cf, 1)

            spread_scores(0)
            spread_scores(1)
            for n in range(NH):
                values(n)
                if n + 2 < NH:
                    spread_scores(n + 2)
            pe.wait_ge(s_rrow, 1)
            for n in range(NH):
                if n >= 2:
                    pe.wait_ge(s_afin, n)
                nc.tensor.matmul(side[:, n % 2, :], sel[:, n, :], mrow[:], start=True, stop=True).then_inc(s_rbc, 1)

            def feed_forward(layer, mixer):
                up, down, ple = f"up{layer}", f"down{layer}", f"ple{layer}"
                chunks(mixer, X)
                sum_acc(mixer)
                chunks(up, X, direct=True)
                chunks(down, (hidH, hidL), fresh=False)
                sum_acc(down)
                chunks(ple, (pxH, pxL), direct=True)

            feed_forward(0, "mout")
            sum_acc("qkv")

            def rotate(st):
                if static(st) and st.k < 3:
                    return
                t = st + -1
                pe.wait_ge(s_read, t.at(TILE0["qkv"] + 1))
                if not static(t) or t.k > 2:
                    pe.wait_ge(s_rotr, t.at(-2))
                for q in range(2):
                    mm = nc.tensor.matmul(side[:, q, 0:HT], perm, u[:, t.k % 2, q * HT:(q + 1) * HT],
                                          start=True, stop=True)
                mm.then_inc(s_rot, 1)

            chunks("qkv", X, extra=rotate, peel=4)
            rotate(Step(0, COUNT["qkv"]))

            for i in range(2):
                if i == 0:
                    pe.wait_ge(s_rope, 2 + KT)
                for b in range(NB):
                    mm = nc.tensor.transpose(side[:, i, b * P:b * P + P], vs[:, i, b * P:b * P + P], ident)
                mm.then_inc(s_vt, 1)
            for i in range(2):
                mm = nc.tensor.transpose(sums[0:DEC, 0, i * P:i * P + P], vs[:, i, SEQ:T], ident)
            mm.then_inc(s_vt, 1)
            def window_scores(gi):
                n, gp = divmod(gi, 4)
                lo = 1 if n == 0 else 0
                if gi >= 2:
                    pe.wait_ge(s_soft, gi - 1)
                for i in range(2):
                    nc.tensor.matmul(tile[gi % 2][:, i, :].rearrange("p (c s) -> p c s", c=2)[:, :, lo * P:],
                                     identR[:], bandR[:, lo * P:].unsqueeze(1).to_broadcast([P, 2, (2 - lo) * P]),
                                     start=True, stop=False, skip_group_check=True)
                for half in range(2):
                    for i in range(2):
                        ti = 2 * gp + i
                        r = slice(HD * half, HD * half + HD)
                        mm = nc.tensor.matmul(tile[gi % 2][:, half, i * 2 * P + lo * P:(i + 1) * 2 * P],
                                              qk[r, 2 + ti, n * P:n * P + P],
                                              qk[r, ti // 4, (n - 1 + lo) * P:(n + 1) * P],
                                              start=False, stop=(i == 1), skip_group_check=True)
                mm.then_inc(s_score, 1)

            def turn(gi):
                lo = 1 if gi < 4 else 0
                pe.wait_ge(s_norm, gi + 1)
                if gi >= 1:
                    pe.wait_ge(s_tua, gi)
                    pe.wait_ge(s_tud, gi)
                for c in range(4):
                    for b in range(lo, 2):
                        mm = nc.tensor.transpose(side[:, c // 2, ((c % 2) * 2 + b) * P:((c % 2) * 2 + b + 1) * P],
                                                 soft[:, gi % 2, c, b * P:b * P + P], ident)
                mm.then_inc(s_tu, 1)

            def weigh(gi):
                n, gp = divmod(gi, 4)
                lo = 1 if n == 0 else 0
                pe.wait_ge(s_tua, gi + 1)
                pe.wait_ge(s_tud, gi + 1)
                if gi >= 2:
                    pe.wait_ge(s_or, gi - 1)
                if gi == 0:
                    pe.wait_ge(s_se, 1)
                if gi == 3:
                    pe.wait_ge(s_sptr, 1)
                if gi == 4:
                    pe.wait_ge(s_satt, 1)
                for c in range(4):
                    half, i = divmod(c, 2)
                    ti = 2 * gp + i
                    head = 2 * (ti // 4) + half
                    for b in range(lo, 2):
                        mm = nc.tensor.matmul(sums[HD * half:HD * half + HD, gi % 2, i * P:i * P + P],
                                              vst[:, n - 1 + b, head * HD:head * HD + HD],
                                              softT[:, gi % 2, c, b * P:b * P + P],
                                              start=(b == lo), stop=(b == 1))
                mm.then_inc(s_pv, 1)

            def sample_scores():
                pe.wait_ge(s_qp, 1)
                pe.wait_ge(s_vtr, 3)
                for c in range(2 * DEC):
                    mm = nc.tensor.matmul(sums[:, 0, 2 * P:3 * P + 1], qpad[:, c, :], kc[:, c // 2, c % 2, :],
                                          start=(c == 0), stop=(c == 2 * DEC - 1))
                mm.then_inc(s_sps, 1)

            def sample_turn():
                pe.wait_ge(s_spn, 2)
                pe.wait_ge(s_or, 2)
                nc.tensor.transpose(sums[:, 1, 2 * P:3 * P], sp[:, 0:P], ident)
                nc.tensor.matmul(sums[:, 1, 3 * P:4 * P], ones, spd[:], start=True, stop=True).then_inc(s_spt, 1)

            def sample_weigh():
                pe.wait_ge(s_sptr, 1)
                pe.wait_ge(s_or, 3)
                for c in range(2 * DEC):
                    b, G = divmod(c, 2)
                    mm = nc.tensor.matmul(sums[:, 0, 2 * P + c * 8:2 * P + c * 8 + 8], vc[:, b, G * P:G * P + P],
                                          spT[:, b * NQ + G * 8:b * NQ + G * 8 + 8], start=True, stop=True)
                mm.then_inc(s_spv, 1)

            groups = 4 * NB
            pe.wait_ge(s_swk, 2)
            window_scores(0)
            window_scores(1)
            sample_scores()
            for gi in range(groups):
                if gi + 2 < groups:
                    window_scores(gi + 2)
                turn(gi)
                if gi >= 1:
                    weigh(gi - 1)
                if gi == 2:
                    sample_turn()
                if gi == 3:
                    sample_weigh()
            weigh(groups - 1)
            feed_forward(1, "sout")

        @block.vector
        def _(dve):
            chain = Chain(dve, s_dve)

            def low(stage, st):
                k, n = slot(stage, st.k), DEPTHK[stage] * P
                dve.wait_ge(s_high, st.at(CHUNK0[stage] + 1))
                nc.vector.tensor_tensor(wL[:, k, 0:n], raw[:, k, 0:n], wH[:, k, 0:n].bitcast(F32),
                                        ALU.subtract).then_inc(s_low, 1)

            def stream(stage, peel, first, then=None):
                def at_window(st):
                    first(st + -1)
                    if st.k + 1 < COUNT[stage] or not static(st):
                        low(stage, st + 1)
                    elif st.k + 1 == COUNT[stage] and following(stage):
                        low(following(stage), Step(0, 0))
                    if then:
                        then(st + -1)
                windows(dve, stage, peel, at_window)

            def second(stage):
                low(stage, Step(0, 1))

            def one_over(stage, dst):
                dve.wait_ge(s_root, NORM[stage] + 1)
                chain.link(nc.vector.reciprocal(dst[:], dst[:]))

            def x_low(stage, k, xh, xl, layer, norm):
                dve.wait_ge(s_xh, XSET[stage] + k + 1)
                nc.vector.scalar_tensor_tensor(out=xl[:, k, :], in0=h[:, k, :], scalar=gains[:, layer, norm, k:k + 1],
                                               in1=xh[:, k, :].bitcast(F32), op0=ALU.mult, op1=ALU.subtract
                                               ).then_inc(s_xr, 1)

            def residual(post, pre, y, layer, g_post, xh, xl, g_pre):
                one_over(post, cg)
                u0 = KT * (2 * layer + (post[:4] == "down"))
                for k in range(KT):
                    if u0 + k >= 2:
                        dve.wait_ge(s_added, u0 + k - 1)
                    nc.vector.scalar_tensor_tensor(
                        out=update[k % 2][:], in0=y[:, k, :], scalar=gains[:, layer, g_post, k:k + 1], in1=cg[:],
                        op0=ALU.mult, op1=ALU.mult).then_inc(s_update, 1)
                    if k:
                        x_low(pre, k - 1, xh, xl, layer, g_pre)
                x_low(pre, KT - 1, xh, xl, layer, g_pre)

            def scaled_read(stage, st, dst, rows=P):
                dve.wait_ge(s_mm, st.at(CHUNK0[stage] + 1))
                nc.vector.tensor_tensor(halves(dst), tile[pslot(stage, st.k)][0:rows, :, 0:HT],
                                        halves(rstd[0:rows, :]), ALU.mult).then_inc(s_read, 1)
                dve.wait_ge(s_read, st.at(TILE0[stage] + 1))

            def copied(stage, y, by):
                def mine(st):
                    return by == 1 or st.k % 2 == 1

                def first(st):
                    if mine(st):
                        o, k = (st.pair, st.k // 2) if by == 2 else (st.at, st.k)
                        dve.wait_ge(s_mm, st.at(CHUNK0[stage] + 1))
                        nc.vector.tensor_scalar(
                            y[:, bass.ds(o(), 1), :].rearrange("p o (q t) -> p (o q) t", q=2),
                            tile[pslot(stage, k)][:, :, 0:HT], 1.0, None, ALU.mult).then_inc(s_yc, 1)

                def then(st):
                    if mine(st):
                        o, k = (st.pair, st.k // 2) if by == 2 else (st.at, st.k)
                        dve.wait_ge(s_read, o(TILE0[stage] + 1))
                        dve.wait_ge(s_acc, o(ON_DVE[stage] + 1))
                        nc.vector.tensor_tensor(acc[:], acc[:], sq[:, k % 2, :], ALU.add).then_inc(s_acc, 1)
                return first, then

            def clear_acc():
                nc.vector.memset(acc[:], 0.0).then_inc(s_acc, 1)

            dve.wait_ge(s_x, 32)
            dve.wait_ge(s_gain, 16)
            dve.wait_ge(s_const, 16)
            low("kv", Step(0, 0))
            for k in range(KT):
                x_low("kv", k, xH, xL, 0, G_PRE_MIX)
            second("kv")
            one_over("kv", rstd)
            fg, ig, ea = u[0:NH, 0, 0:T], cv[0:NH, :], u[0:NH, 1, 0:T]

            def kv_first(st):
                if static(st) and st.k == 0:
                    scaled_read("kv", st, cg[0:GATE2 + NH, :], GATE2 + NH)
                    dve.wait_ge(s_gb, 16)
                    chain.did(nc.vector.tensor_scalar(ig, cg[0:NH, :], gbias[0:NH, 0:1], None, ALU.add))
                    chain.link(nc.vector.tensor_scalar(fg, cg[GATE2:GATE2 + NH, :],
                                                       gbias[GATE2:GATE2 + NH, 0:1], None, ALU.add))
                    nc.vector.scalar_tensor_tensor(out=ea, in0=fg, scalar=-1.0, in1=fg, op0=ALU.mult, op1=ALU.min
                                                   ).then_inc(s_nabs, 1)
                    return
                scaled_read("kv", st, kvq[:, bass.ds(st.at(-1), 1), :].rearrange("p o t -> p (o t)"))

            def kv_then(st):
                if not (static(st) and st.k == 0):
                    return
                dve.wait_ge(s_ln, 1)
                chain.link(nc.vector.scalar_tensor_tensor(out=fg, in0=fg, scalar=0.0, in1=ea, op0=ALU.min,
                                                          op1=ALU.subtract))
                chain.link(nc.vector.tensor_tensor_scan(out=brow[:], data0=ones[0:NH, 0:1].to_broadcast([NH, SEQ]),
                                                        data1=fg[:, 0:SEQ], initial=0.0, op0=ALU.mult, op1=ALU.add))
                chain.link(nc.vector.tensor_tensor(ig[:, 0:SEQ], ig[:, 0:SEQ], brow[:], ALU.subtract))
                chain.link(nc.vector.tensor_tensor_scan(out=mrow[:], data0=ig[:, 0:SEQ], data1=ig[:, 0:SEQ],
                                                        initial=0.0, op0=ALU.max, op1=ALU.max))
                chain.link(nc.vector.tensor_tensor(brow[:], brow[:], mrow[:], ALU.add))
                dve.wait_ge(s_st, 32)
                chain.link(nc.vector.tensor_tensor(srow[:, 0, :], fg[:, SEQ:T], minit[:], ALU.add))
                chain.did(nc.vector.tensor_copy(mout[:, 0:1], brow[:, SEQ - 1:SEQ]))
                chain.link(nc.vector.tensor_tensor(mout[:, 1:], srow[:, 0, :], ig[:, SEQ:T], ALU.max))
                chain.did(nc.vector.tensor_tensor(srow[:, 0, :], srow[:, 0, :], mout[:, 1:], ALU.subtract))
                chain.did(nc.vector.tensor_tensor(srow[:, 1, :], ig[:, SEQ:T], mout[:, 1:], ALU.subtract))
                nc.vector.tensor_scalar(srow[:, 2, :], mout[:, 1:], -1.0, None, ALU.mult).then_inc(s_rows, 1)

            stream("kv", 1, kv_first, kv_then)
            second("qo")
            for i in range(0, 3 * NH):
                if i % 2 == 0:
                    dve.wait_ge(s_turn, i + 1)
                    nc.vector.tensor_copy(turned_to(i)[0], side[:, 0, :].rearrange("p (b c) -> p b c", b=NB)
                                          ).then_inc(s_trd, 1)
                if i % 4 == 3:
                    dve.wait_ge(s_turn, i + 1)
                    dst = (ktoks, vtoks, vtoks)[i // 4][:].rearrange("b n d -> b (n d)")
                    c = (i // 8) * 512
                    nc.vector.tensor_copy(dst[:, c:c + 512], sums[0:DEC, 0, :]).then_inc(s_tsr, 1)
            dve.wait_ge(s_cols, 1)
            chain.did(nc.vector.tensor_copy(acol[:].rearrange("p b n -> p (b n)"), sums[:, 1, 0:16]))
            chain.did(nc.vector.tensor_copy(wscol[:], sums[0:DEC, 1, 16:16 + NH]))
            chain.link(nc.vector.tensor_copy(sbc[:].rearrange("p n a b -> p (n a b)"), sums[:, 1, 32:128]))
            chain.link(nc.vector.tensor_scalar(rs[:, 0, 0:NH], sums[:, 1, 128:128 + NH], 1.0, None, ALU.mult))
            nc.vector.tensor_tensor(wcol[:], acol[:], rs[:, 0, 0:NH].unsqueeze(1).to_broadcast([P, NB, NH]),
                                    ALU.subtract).then_inc(s_dml, 1)
            dve.wait_ge(s_tsr, 3)
            chain.link(nc.vector.tensor_tensor(vtoks[:], vtoks[:], wscol[:].unsqueeze(2).to_broadcast([DEC, NH, DV]),
                                               ALU.mult))

            def qo_first(st):
                d = 3 * NH if st.k < NH and static(st) else 0
                scaled_read("qo", st, kvq[:, bass.ds(st.at(d), 1), :].rearrange("p o t -> p (o t)"))

            def mask(b):
                if not static(b) or b.k >= 2:
                    dve.wait_ge(s_outer, b.at(-1))
                nc.vector.tensor_scalar(vmask[:, b.k % 2], vtoks[:], ident[0:DEC, bass.ds(b.at(), 1)], None, ALU.mult
                                        ).then_inc(s_vm, 1)

            def new_memory(st):
                b = st + -NH
                if static(b) and b.k < 0:
                    return
                if not static(b) or b.k + 1 < DEC:
                    mask(b + 1)
                dve.wait_ge(s_cin[b.k % 2], 16 * b.pair(1))
                dve.wait_ge(s_outer, b.at(1))
                for n in range(NH):
                    last = nc.vector.scalar_tensor_tensor(
                        out=cring[:, b.k % 2, n, :], in0=cring[:, b.k % 2, n, :],
                        scalar=sbc[:, n, 0, bass.ds(b.at(), 1)],
                        in1=side[:, n // 2, (n % 2) * DV:(n % 2 + 1) * DV], op0=ALU.mult, op1=ALU.add)
                last.then_inc(s_cnew, 1)

            mask(Step(0, 0))
            stream("qo", NH + 2, qo_first, new_memory)
            second("mout")

            wold, wnew = sbc[:, :, 0, :], sbc[:, :, 1, :]
            chain.did(nc.vector.tensor_tensor(nst[:], nst[:], wold, ALU.mult))
            chain.link(nc.vector.tensor_tensor(ntmp[:, 0], kvq[:, 0:NH, SEQ:T], wnew, ALU.mult))
            chain.link(nc.vector.tensor_tensor(nst[:], nst[:], ntmp[:, 0], ALU.add))
            nc.vector.tensor_tensor(ntmp[:, 0], nst[:], kvq[:, 3 * NH:4 * NH, SEQ:T], ALU.mult).then_inc(s_prod, 1)
            dve.wait_ge(s_qns, 1)
            flat_rs = rs[:].rearrange("p n b -> p (n b)")
            chain.link(nc.vector.tensor_scalar(flat_rs, sums[:, 1, P:P + NH * DEC], DK_SCALE, None, ALU.mult))
            chain.link(nc.vector.scalar_tensor_tensor(out=flat_rs, in0=flat_rs, scalar=-1.0, in1=flat_rs,
                                                      op0=ALU.mult, op1=ALU.max))
            chain.link(nc.vector.tensor_tensor(rs[:], rs[:], sbc[:, :, 2, :], ALU.max))
            chain.link(nc.vector.reciprocal(rs[:], rs[:]))
            dve.wait_ge(s_snum, DEC)
            for half in range(2):
                chain.did(nc.vector.tensor_tensor(
                    stmp[:, :, half, :], sums[:, 1, 0:KT * DEC].rearrange("p (n e b) -> p n e b", n=NH, e=2)[:, :, half, :],
                    rs[:], ALU.mult))
            dve.wait_ge(s_dve, chain.n)
            dve.wait_ge(s_sigo, 2)
            osamp = kvq[:, NH:3 * NH, SEQ:T]
            nc.vector.scalar_tensor_tensor(out=osamp, in0=stmp[:].rearrange("p n e b -> p (n e) b"), scalar=DK_SCALE,
                                           in1=osamp, op0=ALU.mult, op1=ALU.mult).then_inc(s_afin, 1)

            def diag(n):
                dve.wait_ge(s_mb, n + 1)
                if n >= 1:
                    dve.wait_ge(s_expd, n)
                nc.vector.scalar_tensor_tensor(
                    out=cg[:, 0:SEQ].rearrange("p (b t) -> p b t", b=NB),
                    in0=sums[:, 0, :].rearrange("p (b t) -> p b t", b=NB), scalar=-1.0,
                    in1=causal.unsqueeze(1).to_broadcast([P, NB, P]), op0=ALU.mult, op1=ALU.add).then_inc(s_diag, 1)

            def weights(n):
                dve.wait_ge(s_expd, n + 1)
                dve.wait_ge(s_score, n + 1)
                at0 = 0
                for j in range(NB):
                    b, c = ((0, 0), (0, 512), (1, 0), (1, 256))[j]
                    w = SEQ - j * P
                    pj = prob[:, n % 2, at0:at0 + w]
                    last = nc.vector.scalar_tensor_tensor(
                        out=pj, in0=tile[b][:].rearrange("p q t -> p (q t)")[:, c:c + w], scalar=DK_SCALE, in1=pj,
                        op0=ALU.mult, op1=ALU.mult)
                    at0 += w
                last.then_inc(s_prob, 1)

            def final_weights(n):
                if n == 0:
                    dve.wait_ge(s_wcol, 1)
                else:
                    dve.wait_ge(s_cf, n)
                nc.vector.tensor_tensor(kw, ktok[:, :, n, :], wcol[:, :, n:n + 1].to_broadcast([P, NB, P]),
                                        ALU.mult).then_inc(s_kw, 1)

            diag(0)
            weights(0)
            diag(1)
            final_weights(0)
            for n in range(NH):
                if n + 1 < NH:
                    weights(n + 1)
                dve.wait_ge(s_num, n + 1)
                for half in range(2):
                    o = kvq[:, NH + 2 * n + half, 0:SEQ]
                    last = nc.vector.tensor_tensor(o, side[:, half, :], o, ALU.mult)
                last.then_inc(s_nr, 1)
                dve.wait_ge(s_cf, n + 1)
                nc.vector.tensor_copy(cfin[:, n, :], sums[:, 1, 0:DV + 1]).then_inc(s_cfr, 1)
                if n + 1 < NH:
                    final_weights(n + 1)
                if n + 2 < NH:
                    diag(n + 2)
            chain.link(nc.vector.scalar_tensor_tensor(out=mrow[:], in0=tile[1][0:NH, 1, :], scalar=-1.0,
                                                      in1=erow, op0=ALU.mult, op1=ALU.max))
            chain.link(nc.vector.tensor_tensor(mrow[:], tile[1][0:NH, 1, :], mrow[:], ALU.max))
            nc.vector.reciprocal(mrow[:], mrow[:]).then_inc(s_rrow, 1)
            clear_acc()

            def o_low(k):
                dve.wait_ge(s_xh, XSET["mout"] + k + 1)
                nc.vector.tensor_tensor(xL[:, k, :], o_tile(k), xH[:, k, :].bitcast(F32), ALU.subtract).then_inc(s_xr, 1)

            dve.wait_ge(s_nr, NH)
            for n in range(NH):
                dve.wait_ge(s_rbc, n + 1)
                o = kvq[:, NH + 2 * n:NH + 2 * n + 2, 0:SEQ]
                nc.vector.tensor_tensor(o, o, side[:, n % 2, :].unsqueeze(1).to_broadcast([P, 2, SEQ]), ALU.mult
                                        ).then_inc(s_afin, 1)
                if n:
                    o_low(2 * n - 2)
                    o_low(2 * n - 1)
            o_low(KT - 2)
            o_low(KT - 1)

            def feed_forward(layer, mixer, y):
                up, down, ple = f"up{layer}", f"down{layer}", f"ple{layer}"
                stream(mixer, 2, *copied(mixer, y, 1))
                second(up)
                residual(mixer, up, y, layer, G_POST_MIX, xH, xL, G_PRE_FFN)
                dve.wait_ge(s_cw, 32 * (layer + 1))
                dve.wait_ge(s_pad, layer + 1)
                for j in range(CW - 1):
                    chain.did(nc.vector.tensor_tensor(prev[:, :, j, :], prev[:, :, j, :],
                                                      convw[:, :, j:j + 1].to_broadcast([P, UP, DEC]), ALU.mult))
                dve.wait_ge(s_dve, chain.n)
                chain.link(nc.vector.tensor_tensor(prev[:, :, 0, :], prev[:, :, 0, :], prev[:, :, 1, :], ALU.add))
                one_over(up, rstd)

                def read_up(st):
                    if not static(st) or st.k > 1:
                        dve.wait_ge(s_cc, st.at(UP * layer - 1))
                    nc.vector.tensor_scalar(taps[:, st.k % 2, :], convw[:, bass.ds(st.at(), 1), :]
                                            .rearrange("p o c -> p (o c)"), 1.0, None, ALU.mult)
                    scaled_read(up, st, u[:, st.k % 2, 2:])

                def conv(st):
                    r, c = st.k % 2, (cg, cv)[st.k % 2]
                    ur = u[:, r, :]
                    t = bass.ds(st.at(), 1)
                    nc.vector.tensor_scalar(newrows[:, t, :].rearrange("p o c -> p (o c)"), ur[:, SEQ:], 1.0, None,
                                            ALU.mult)
                    dve.wait_ge(s_ca, st.at(UP * layer + 1))
                    nc.vector.tensor_tensor(c[:, SEQ:], c[:, SEQ:], prev[:, t, 0, :].rearrange("p o c -> p (o c)"),
                                            ALU.add)
                    nc.vector.scalar_tensor_tensor(out=c[:, 0:SEQ], in0=ur[:, 1:SEQ + 1], scalar=taps[:, r, 1:2],
                                                   in1=c[:, 0:SEQ], op0=ALU.mult, op1=ALU.add).then_inc(s_c1, 1)
                    if r == 0 and (not static(st) or st.k):
                        hid_low((st + -1).pair)
                    dve.wait_ge(s_c1, st.at(UP * layer + 1))
                    nc.vector.scalar_tensor_tensor(out=c[:, 0:SEQ], in0=ur[:, 0:SEQ], scalar=taps[:, r, 0:1],
                                                   in1=c[:, 0:SEQ], op0=ALU.mult, op1=ALU.add).then_inc(s_cc, 1)
                    if r:
                        dve.wait_ge(s_silu, st.pair(FT * layer + 1))
                        dve.wait_ge(s_cc, st.at(UP * layer + 1))
                        nc.vector.tensor_tensor(cv[:], cg[:], cv[:], ALU.mult).then_inc(s_gated, 1)

                def hid_low(p):
                    hH = hidH[:, bass.ds(p(), 1), :].rearrange("p o t -> p (o t)")
                    hL = hidL[:, bass.ds(p(), 1), :].rearrange("p o t -> p (o t)")
                    dve.wait_ge(s_hh, p(FT * layer + 1))
                    nc.vector.tensor_tensor(hL, cv[:], hH.bitcast(F32), ALU.subtract).then_inc(s_hid, 1)

                stream(up, 2, read_up, conv)
                hid_low(Step(0, UP - 1).pair)
                second(down)
                clear_acc()
                stream(down, 2, *copied(down, y_down, 2))
                second(ple)
                residual(down, ple, y_down, layer, G_POST_FFN, pxH, pxL, G_PLE)
                dve.wait_ge(s_ph, layer + 1)
                nc.vector.tensor_tensor(pL[:], pin[:], pH[:].bitcast(F32), ALU.subtract).then_inc(s_pr, 1)
                if layer + 1 < NL:
                    clear_acc()
                one_over(ple, rstd)

                def embed(st):
                    scaled_read(ple, st, cg[:])

                def add_embed(st):
                    n = KT * layer
                    dve.wait_ge(s_sig, st.at(n + 1))
                    nc.vector.tensor_tensor(halves(cv[:]), halves(cg[:]), side[:, :, 0:HT], ALU.mult).then_inc(s_side, 1)
                    dve.wait_ge(s_side, st.at(n + 1))
                    o = bass.ds(st.at(), 1)
                    ht = h[:, o, :].rearrange("p o t -> p (o t)")
                    nc.vector.tensor_tensor(ht, ht, cv[:], ALU.add).then_inc(s_h, 1)
                    if layer + 1 == NL:
                        return
                    dve.wait_ge(s_h, st.at(KT * layer + 1))
                    gain = gains[:, layer + 1, G_PRE_MIX, o]
                    xh, xl = (x[:, o, :].rearrange("p o t -> p (o t)") for x in (xH, xL))
                    nc.vector.tensor_scalar(xh, ht, gain, None, ALU.mult).then_inc(s_xh, 1)
                    nc.vector.tensor_tensor(cv[:], ht, ht, ALU.mult).then_inc(s_psq, 1)
                    dve.wait_ge(s_xh, st.at(XSET["qkv"] + 1))
                    nc.vector.scalar_tensor_tensor(out=xl, in0=ht, scalar=gain, in1=xh.bitcast(F32),
                                                   op0=ALU.mult, op1=ALU.subtract).then_inc(s_xr, 1)
                    dve.wait_ge(s_psq, st.at(1))
                    dve.wait_ge(s_acc, st.at(ON_DVE["qkv"] + 1))
                    nc.vector.tensor_tensor(acc[:], acc[:], cv[:], ALU.add).then_inc(s_acc, 1)

                stream(ple, 2, embed, add_embed)

            feed_forward(0, "mout", y_ml)

            second("qkv")
            one_over("qkv", rstd)
            dve.wait_ge(s_swc, 16 * 5)
            chain.link(nc.vector.tensor_scalar(sinks[:], sinks[:], -1.0, None, ALU.mult))

            def qkv_first(st):
                if static(st) and st.k < 2:
                    scaled_read("qkv", st, vs[:, st.k, :])
                else:
                    scaled_read("qkv", st, u[:, st.k % 2, 0:T])

            def rope(st):
                if static(st) and st.k < 3:
                    return
                t = st + -1
                d = qk[:, bass.ds(t.at(-2), 1), :].rearrange("p o t -> p (o t)")
                dve.wait_ge(s_rot, t.at(-1))
                if not static(t) or t.k > 2:
                    dve.wait_ge(s_rope, t.at(-2))
                nc.vector.tensor_tensor(cg[:], u[:, t.k % 2, 0:T], cos_t[:], ALU.mult)
                nc.vector.tensor_tensor(halves(cv[:]), side[:, :, 0:HT], halves(sin_t[:]), ALU.mult).then_inc(s_rotr, 1)
                dve.wait_ge(s_rotr, t.at(-1))
                nc.vector.tensor_tensor(d, cg[:], cv[:], ALU.add).then_inc(s_rope, 1)

            stream("qkv", 4, qkv_first, rope)
            rope(Step(0, COUNT["qkv"]))
            second("sout")
            for i in range(2):
                dve.wait_ge(s_vt, i + 1)
                nc.vector.tensor_copy(vst[:, :, i * P:i * P + P], side[:, i, :].rearrange("p (b c) -> p b c", b=NB)
                                      ).then_inc(s_vtr, 1)
            dve.wait_ge(s_vt, 3)
            nc.vector.tensor_copy(vnew[:], sums[0:DEC, 0, 0:2 * P]).then_inc(s_vtr, 1)
            dve.wait_ge(s_rope, 2 + KT)
            dve.wait_ge(s_qz, 1)
            nc.vector.tensor_copy(kc[:, :, :, WINDOW], qk[:, 0:2, SEQ:T].rearrange("p g b -> p b g"))
            flat = qpad[:].rearrange("p c m -> p (c m)")
            for ti in range(KT):
                G, j = divmod(ti, 4)
                for half in range(2):
                    r = slice(HD * half, HD * half + HD)
                    c0 = G * P + G * 8 + half * 4 + j
                    step = 2 * P + NQ
                    last = nc.vector.tensor_copy(flat[r, c0:c0 + 7 * step + 1:step], qk[r, 2 + ti, SEQ:T])
            last.then_inc(s_qp, 1)
            nsink = sinks[:, NQ:NQ + 1]
            c4 = cv[:, 0:P].rearrange("p (b g e) -> p b g e", b=DEC, g=2)

            def sample_shift():
                dve.wait_ge(s_sps, 1)
                chain.link(nc.vector.tensor_reduce(sst[:, 0:1], sums[:, 0, 2 * P:3 * P + 1], AXX, ALU.max, negate=True))
                chain.link(nc.vector.scalar_tensor_tensor(out=sst[:, 1:2], in0=sst[:, 0:1], scalar=QK_SCALE, in1=nsink,
                                                          op0=ALU.mult, op1=ALU.min))
                nc.vector.tensor_tensor(sst[:, 2:3], sst[:, 1:2], nsink, ALU.subtract).then_inc(s_sz, 1)

            def sample_normalise():
                dve.wait_ge(s_se, 2)
                chain.link(nc.vector.tensor_tensor(sst[:, 5:6], sst[:, 3:4], sst[:, 4:5], ALU.add))
                chain.link(nc.vector.reciprocal(sst[:, 6:7], sst[:, 5:6]))
                nc.vector.tensor_scalar(sp[:], sp[:], sst[:, 6:7], None, ALU.mult).then_inc(s_spn, 1)
                dve.wait_ge(s_spn, 1)
                nc.vector.tensor_scalar(spd[:], ident, sp[:, WINDOW:WINDOW + 1], None, ALU.mult).then_inc(s_spn, 1)

            def sample_turn_read():
                dve.wait_ge(s_spt, 1)
                nc.vector.tensor_copy(spT[:], sums[:, 1, 2 * P:4 * P]).then_inc(s_sptr, 1)
                dve.wait_ge(s_sptr, 1)
                for G in range(2):
                    chain.did(nc.vector.tensor_tensor(
                        c4[:, :, G, :], spT[:, P:2 * P].rearrange("p (b g e) -> p b g e", b=DEC, g=2)[:, :, G, :],
                        vs[:, G, SEQ:T].unsqueeze(2).to_broadcast([P, DEC, 8]), ALU.mult))
                dve.wait_ge(s_dve, chain.n)

            def sample_attention():
                dve.wait_ge(s_spv, 1)
                chain.link(nc.vector.tensor_tensor(cv[:, 0:P], cv[:, 0:P], sums[:, 0, 2 * P:3 * P], ALU.add))
                for half in range(2):
                    r = slice(HD * half, HD * half + HD)
                    for G in range(2):
                        last = nc.vector.tensor_copy(att[r, 4 * G:4 * G + 4, SEQ:T],
                                                     c4[r, :, G, 4 * half:4 * half + 4].rearrange("p b j -> p j b"))
                last.then_inc(s_satt, 1)

            def shift(gi):
                gp, k = gi % 4, gi % 2
                w0 = P if gi < 4 else 0
                dve.wait_ge(s_score, NH + gi + 1)
                if gi >= 2:
                    dve.wait_ge(s_norm, gi - 1)
                chain.link(nc.vector.tensor_reduce(
                    sm[:, k, 0, :], tile[k][:].rearrange("p i (c s) -> p (i c) s", c=2)[:, :, w0:], AXX, ALU.max,
                    negate=True))
                ns = sinks[:, 4 * gp:4 * gp + 4]
                chain.link(nc.vector.scalar_tensor_tensor(out=sm[:, k, 0, :], in0=sm[:, k, 0, :], scalar=QK_SCALE,
                                                          in1=ns, op0=ALU.mult, op1=ALU.min))
                nc.vector.tensor_tensor(sm[:, k, 1, :], sm[:, k, 0, :], ns, ALU.subtract).then_inc(s_z, 1)

            def normalise(gi):
                k = gi % 2
                w0 = P if gi < 4 else 0
                dve.wait_ge(s_soft, gi + 1)
                chain.link(nc.vector.tensor_tensor(sm[:, k, 3, :], sm[:, k, 3, :], sm[:, k, 2, :], ALU.add))
                chain.link(nc.vector.reciprocal(sm[:, k, 3, :], sm[:, k, 3, :]))
                for c in range(4):
                    last = nc.vector.tensor_scalar(soft[:, k, c, w0:], soft[:, k, c, w0:], sm[:, k, 3, c:c + 1], None,
                                                   ALU.mult)
                last.then_inc(s_norm, 1)

            def turn_read(gi):
                dve.wait_ge(s_tu, gi + 1)
                if gi >= 2:
                    dve.wait_ge(s_pv, gi - 1)
                lo = 1 if gi < 4 else 0
                nc.vector.tensor_copy(softT[:, gi % 2, 2:4, lo * P:].rearrange("p c (b t) -> p c b t", t=P),
                                      side[:, 1, :].rearrange("p (c b t) -> p c b t", c=2, b=2)[:, :, lo:, :]
                                      ).then_inc(s_tud, 1)

            groups = 4 * NB

            def x_low_att(gp):
                for k in (2 * gp, 2 * gp + 1):
                    dve.wait_ge(s_xh, XSET["sout"] + k + 1)
                    nc.vector.tensor_tensor(xL[:, k, :], att[:, k, :], xH[:, k, :].bitcast(F32), ALU.subtract
                                            ).then_inc(s_xr, 1)

            shift(0)
            for gi in range(groups):
                if gi + 1 < groups:
                    shift(gi + 1)
                normalise(gi)
                turn_read(gi)
                if gi < 4:
                    (sample_shift, sample_normalise, sample_turn_read, sample_attention)[gi]()
                if gi == groups - 1:
                    clear_acc()
                if gi >= groups - 2:
                    x_low_att(gi - (groups - 2))
            x_low_att(2)
            x_low_att(3)
            dve.wait_ge(s_out, 16 * STORED_L0)
            feed_forward(1, "sout", y_sw)


def _weight_chunks(np, w, groups):
    k = w.shape[0] // P
    wide = np.concatenate([w, np.zeros((w.shape[0], 1), w.dtype)], axis=1)
    c = wide[:, np.asarray(groups).reshape(-1)].reshape(k, P, len(groups), P)
    return np.ascontiguousarray(c.transpose(2, 1, 0, 3).reshape(len(groups), P, k * P))


def _features(np, x):
    return np.ascontiguousarray(x.T.reshape(-1, P, x.shape[0]).transpose(1, 0, 2))


def _constants(np):
    c = np.zeros((P, C_ALL), np.float32)
    r = np.arange(P)
    c[:, C_IDENT:C_IDENT + P] = np.eye(P)
    c[:, C_ONES:C_ONES + P] = 1.0
    c[:, C_CAUSAL:C_CAUSAL + P] = np.where(r[None, :] >= r[:, None], 0.0, NEG)
    c[r, C_PERM + (r ^ (HD // 2))] = 1.0
    c[:, C_BAND:C_BAND + P] = np.where(r[None, :] >= r[:, None], 0.0, NEG)
    c[:, C_BAND + P:C_BAND + 2 * P] = np.where(r[None, :] <= r[:, None], 0.0, NEG)
    for n in range(NH):
        c[n, C_SEL + n * P:C_SEL + n * P + P] = 1.0
        c[:, C_HOT + n * NH + n] = 1.0
    half = HD // 2
    inv = np.float32(THETA) ** (-np.arange(half, dtype=np.float32) / np.float32(half))
    pos = np.concatenate([np.arange(SEQ), np.full(DEC, PAST)]).astype(np.float32)
    ang = inv.astype(np.float32)[r % half][:, None] * pos[None, :]
    sign = np.where(r % HD < half, -1.0, 1.0).astype(np.float32)[:, None]
    return c, np.cos(ang).astype(np.float32), (np.sin(ang) * sign).astype(np.float32)


def kernel(**inputs):
    import numpy as np
    from types import SimpleNamespace
    import concourse.bacc as bacc
    from concourse.bass_utils import run_bass_kernel_spmd

    a = {k: np.asarray(v) for k, v in inputs.items()}
    run = np.arange(P)
    seq = lambda first, n: [first + P * i + run for i in range(n)]
    both = lambda x, y: _features(np, np.concatenate([x, y], axis=0))

    hk = NH * P
    gates = np.full(P, -1)
    gates[0:NH] = 2 * hk + 2 * D + np.arange(NH)
    gates[GATE2:GATE2 + NH] = 2 * hk + 2 * D + NH + np.arange(NH)
    kv = [gates] + seq(hk, NH) + seq(2 * hk, KT)
    qo = seq(0, NH) + seq(2 * hk + D, KT)
    order = [(2 * G + half) * NG + j for G in range(2) for j in range(NG) for half in range(2)]
    qcols = np.concatenate([hd * HD + np.arange(HD) for hd in order])
    qkv = seq((NQ + NKV) * HD, 2) + seq(NQ * HD, 2) + list(qcols.reshape(KT, P))
    w_in, w_sw = a["ml_w_in"][0], a["sw_w_in"][0]
    data = {
        "w_kv": _weight_chunks(np, w_in, kv), "w_qo": _weight_chunks(np, w_in, qo),
        "w_mout": _weight_chunks(np, a["ml_w_out"][0], seq(0, KT)),
        "w_qkv": _weight_chunks(np, w_sw, qkv),
        "w_sout": _weight_chunks(np, a["sw_w_out"][0][qcols], seq(0, KT)),
    }
    updown = [c for i in range(FT) for c in (P * i + run, FT * P + P * i + run)]
    for layer in range(NL):
        data[f"w_up{layer}"] = _weight_chunks(np, a["ffn_w_up"][layer], updown)
        dn = _weight_chunks(np, a["ffn_w_down"][layer], seq(0, KT))
        data[f"w_down{layer}"] = np.ascontiguousarray(
            dn.reshape(KT, P, 2, DKH * P).transpose(0, 2, 1, 3).reshape(2 * KT, P, DKH * P))
        data[f"w_ple{layer}"] = _weight_chunks(
            np, np.concatenate([a["ple_w_gate"][layer], a["ple_w_proj"][layer]], axis=0), seq(0, KT))
    data["x"] = both(a["x_prompt"][0], a["x_sample"][:, 0])
    data["p"] = np.stack([both(a["p_prompt"][i, 0], a["p_sample"][i, :, 0]) for i in range(NL)])
    data["gains"] = np.ascontiguousarray(np.stack(
        [a[n] for n in ("g_pre_mix", "g_post_mix", "g_pre_ffn", "g_post_ffn", "g_ple")], axis=1
    ).reshape(NL, 5, KT, P).transpose(3, 0, 1, 2))
    gb = np.zeros((GATE2 + NH, 1), np.float32)
    gb[0:NH, 0], gb[GATE2:, 0] = a["ml_b_gate"][0, :NH], a["ml_b_gate"][0, NH:]
    data["gate_bias"] = gb
    data["c_in"] = np.ascontiguousarray(a["state_mlstm_C"][0].transpose(0, 2, 1, 3))
    data["n_in"] = np.ascontiguousarray(a["state_mlstm_n"][0].transpose(2, 1, 0))
    data["m_in"] = np.ascontiguousarray(a["state_mlstm_m"][0].T)
    data["kc_in"] = np.ascontiguousarray(
        a["cache_swa_k"][0].reshape(DEC, WINDOW, 2, 2, HD).transpose(3, 4, 0, 2, 1).reshape(P, DEC, 2, WINDOW))
    data["vc_in"] = np.ascontiguousarray(a["cache_swa_v"][0].reshape(DEC, WINDOW, NKV * HD).transpose(1, 0, 2))
    data["conv_prev"] = np.ascontiguousarray(
        a["state_conv"].reshape(NL, DEC, CW - 1, 2, FT, P).transpose(0, 5, 4, 3, 2, 1).reshape(NL, P, UP, CW - 1, DEC))
    taps = np.concatenate([a["ffn_conv_w"], a["ffn_conv_b"][:, None]], axis=1)
    data["convw"] = np.ascontiguousarray(
        taps.reshape(NL, CW + 1, 2, FT, P).transpose(0, 4, 3, 2, 1).reshape(NL, P, UP, CW + 1))
    sk = a["sw_sinks"][0]
    groups = [order[4 * gp + 2 * i + half] for gp in range(NQ // 4) for half in range(2) for i in range(2)]
    data["sinks"] = np.ascontiguousarray(np.concatenate(
        [np.broadcast_to(sk[groups], (P, NQ)), np.tile(sk, DEC)[:, None]], axis=1))
    data["const"], data["cos_t"], data["sin_t"] = _constants(np)

    outs = {"y": (P, KT, T), "c_p": (P, NH, DV + 1), "m_all": (NH, 1 + DEC), "k_p": (P, 2, WINDOW),
            "v_p": (P, 2, WINDOW), "newrows": (NL, P, UP, 2 + DEC), "conv_old": (NL, P, UP, DEC),
            "c_s": (DEC, P, NH, DV), "n_s": (P, NH, DEC), "k_s": (P, DEC, 2, WINDOW),
            "v_s": (WINDOW, DEC, NKV * HD)}
    nc = bacc.Bacc("TRN2", target_bir_lowering=False, num_devices=1)
    aps = {k: nc.dram_tensor(f"in_{k}", v.shape, mybir.dt.from_np(v.dtype), kind="ExternalInput").ap()
           for k, v in data.items()}
    aps.update({k: nc.dram_tensor(f"out_{k}", v, F32, kind="ExternalOutput").ap() for k, v in outs.items()})
    aps["weights"] = {s: aps[f"w_{s}"] for s in ORDER}
    build(nc, SimpleNamespace(**aps))
    r = run_bass_kernel_spmd(nc, [{f"in_{k}": v for k, v in data.items()}], core_ids=[0]).results[0]
    o = {k: r[f"out_{k}"] for k in outs}

    y = o["y"].transpose(2, 1, 0).reshape(T, D)
    rows = o["newrows"].reshape(NL, P, FT, 2, 2 + DEC).transpose(0, 4, 3, 2, 1).reshape(NL, 2 + DEC, UP * P)
    old = o["conv_old"].reshape(NL, P, FT, 2, DEC).transpose(0, 4, 3, 2, 1).reshape(NL, DEC, UP * P)
    heads = lambda x: x.reshape(2, HD, 2, WINDOW).transpose(3, 2, 0, 1).reshape(1, 1, WINDOW, NKV, HD)
    outputs = (
        y[None, :SEQ], y[SEQ:, None],
        o["c_p"][:, :, :DV].transpose(1, 0, 2)[None, None], o["c_p"][:, :, DV].T[None, None], o["m_all"][None, None, :, 0],
        heads(o["k_p"]), heads(o["v_p"]), rows[:, None, 0:2],
        o["c_s"].transpose(0, 2, 1, 3)[None], o["n_s"].transpose(2, 1, 0)[None], o["m_all"][:, 1:].T[None],
        o["k_s"].reshape(2, HD, DEC, 2, WINDOW).transpose(2, 4, 3, 0, 1).reshape(1, DEC, WINDOW, NKV, HD),
        o["v_s"].transpose(1, 0, 2).reshape(1, DEC, WINDOW, NKV, HD),
        np.stack([old, rows[:, 2:]], axis=2),
    )
    return tuple(np.ascontiguousarray(x) for x in outputs)
```
